# Optimizing a Trainium2 kernel written in Bass

```python
import jax, jax.numpy as jnp
from jax import lax
import numpy as np

D_MODEL = 1024
BATCH = 1
SEQ = 256
DEPTH = 1

CHUNK = 64
Q_BLOCK = 128
EPS = 1e-6

CONV_WIDTH = D_MODEL
CONV_K = 3

N_HEADS = D_MODEL // 128
QK_NOPE = 128
QK_ROPE = 64
QK_HEAD = QK_NOPE + QK_ROPE
V_HEAD = D_MODEL // N_HEADS
Q_LORA = (3 * D_MODEL) // 8
KV_LORA = D_MODEL // 4
ROPE_BASE = 10000.0

COL_SIZES = (CONV_WIDTH, CONV_WIDTH, CONV_WIDTH, Q_LORA, KV_LORA, QK_ROPE, D_MODEL, D_MODEL)
D_IN_ALL = sum(COL_SIZES)
COL_SPLITS = tuple(int(v) for v in np.cumsum(COL_SIZES)[:-1])

N_GROUPS = 4
EXPERTS_PER_GROUP = 8
N_EXPERTS = N_GROUPS * EXPERTS_PER_GROUP
TOP_K = 2
D_EXPERT = D_MODEL // 4

kernel_name = 'hybrid_conv_mla_hmoe_block'

def rms_norm(x, g):
    xf = x.astype(jnp.float32)
    y = xf * lax.rsqrt(jnp.mean(xf * xf, axis=-1, keepdims=True) + EPS)
    return (y * g.astype(jnp.float32)).astype(x.dtype)

def rope_tables(positions):
    inv = ROPE_BASE ** (-jnp.arange(0, QK_ROPE, 2, dtype=jnp.float32) / QK_ROPE)
    ang = positions.astype(jnp.float32)[..., None] * inv
    return jnp.cos(ang)[:, :, None, :], jnp.sin(ang)[:, :, None, :]

def apply_rope(x, cos, sin):
    xf = x.astype(jnp.float32)
    x1, x2 = xf[..., :QK_ROPE // 2], xf[..., QK_ROPE // 2:]
    out = jnp.concatenate([x1 * cos - x2 * sin, x2 * cos + x1 * sin], axis=-1)
    return out.astype(x.dtype)

def short_causal_conv(u, w):
    S = u.shape[1]
    up = jnp.pad(u, ((0, 0), (CONV_K - 1, 0), (0, 0)))
    y = up[:, 0:S] * w[0]
    for k in range(1, CONV_K):
        y = y + up[:, k:k + S] * w[k]
    return y

def chunk_causal_attention(q, k, v):
    S = q.shape[1]
    scale = QK_HEAD ** -0.5
    outs = []
    for i in range(S // Q_BLOCK):
        q0 = i * Q_BLOCK
        kend = q0 + Q_BLOCK
        qb = q[:, q0:kend]
        kb = k[:, :kend]
        vb = v[:, :kend]
        s = jnp.einsum('bqhd,bkhd->bhqk', qb, kb).astype(jnp.float32) * scale
        q_chunk = (q0 + jnp.arange(Q_BLOCK)) // CHUNK
        k_chunk = jnp.arange(kend) // CHUNK
        mask = k_chunk[None, :] <= q_chunk[:, None]
        s = jnp.where(mask, s, jnp.finfo(jnp.float32).min)
        p = jax.nn.softmax(s, axis=-1).astype(v.dtype)
        outs.append(jnp.einsum('bhqk,bkhd->bqhd', p, vb))
    return jnp.concatenate(outs, axis=1)

def mla_branch(q_lat, kv_lat, k_rope_raw, cos, sin, q_a_norm_g, w_q_b, kv_a_norm_g, w_kv_b, q_norm_g, k_norm_g):
    B, S = q_lat.shape[0], q_lat.shape[1]
    q = (rms_norm(q_lat, q_a_norm_g) @ w_q_b).reshape(B, S, N_HEADS, QK_HEAD)
    q = rms_norm(q, q_norm_g)
    q = jnp.concatenate([q[..., :QK_NOPE], apply_rope(q[..., QK_NOPE:], cos, sin)], axis=-1)
    kv = (rms_norm(kv_lat, kv_a_norm_g) @ w_kv_b).reshape(B, S, N_HEADS, QK_NOPE + V_HEAD)
    k_nope, v = kv[..., :QK_NOPE], kv[..., QK_NOPE:]
    k_rope = jnp.broadcast_to(k_rope_raw[:, :, None, :], (B, S, N_HEADS, QK_ROPE))
    k = rms_norm(jnp.concatenate([k_nope, k_rope], axis=-1), k_norm_g)
    k = jnp.concatenate([k[..., :QK_NOPE], apply_rope(k[..., QK_NOPE:], cos, sin)], axis=-1)
    o = chunk_causal_attention(q, k, v)
    return o.reshape(B, S, N_HEADS * V_HEAD)

def hierarchical_moe(h, w_rg, b_rg, w_re, b_re, w_gate, w_up, w_down):
    B, S = h.shape[0], h.shape[1]
    g_logits = (h @ w_rg).astype(jnp.float32) + b_rg.astype(jnp.float32)
    g_prob = jax.nn.softmax(g_logits, axis=-1)
    g_onehot = jax.nn.one_hot(jnp.argmax(g_logits, axis=-1), N_GROUPS, dtype=jnp.float32)
    p_group = jnp.sum(g_prob * g_onehot, axis=-1)
    e_logits = ((h @ w_re).astype(jnp.float32) + b_re.astype(jnp.float32)).reshape(B, S, N_GROUPS, EXPERTS_PER_GROUP)
    e_sel = jnp.sum(e_logits * g_onehot[..., None], axis=-2)
    e_prob = jax.nn.softmax(e_sel, axis=-1)
    top_v, top_i = lax.top_k(e_prob, TOP_K)
    top_v = top_v / jnp.sum(top_v, axis=-1, keepdims=True)
    w_local = jnp.sum(jax.nn.one_hot(top_i, EXPERTS_PER_GROUP, dtype=jnp.float32) * top_v[..., None], axis=-2)
    comb = (g_onehot[..., :, None] * w_local[..., None, :] * p_group[..., None, None]).astype(h.dtype)
    out = jnp.zeros_like(h)
    for g in range(N_GROUPS):
        a = jax.nn.silu(jnp.einsum('bsd,edf->bsef', h, w_gate[g])) * jnp.einsum('bsd,edf->bsef', h, w_up[g])
        a = a * comb[:, :, g, :, None]
        out = out + jnp.einsum('bsef,efd->bsd', a, w_down[g])
    return out

def setup_inputs(seed: int = 0) -> dict:
    key = jax.random.key(seed)
    ks = jax.random.split(key, 24)
    f32 = jnp.float32
    nrm = lambda k, shape, s: jax.random.normal(k, shape, f32) * s
    L = DEPTH
    x = jax.random.normal(ks[0], (BATCH, SEQ, D_MODEL), f32)
    c = jax.random.normal(ks[1], (BATCH, D_MODEL), f32)
    offsets = jax.random.randint(ks[2], (BATCH, 1), 0, 4096, dtype=jnp.int32)
    positions = (offsets + jnp.arange(SEQ, dtype=jnp.int32)[None, :]).astype(jnp.int32)
    return {
        'x': x,
        'c': c,
        'positions': positions,
        'w_ada': nrm(ks[3], (L, D_MODEL, 6 * D_MODEL), D_MODEL ** -0.5),
        'b_ada': nrm(ks[4], (L, 6 * D_MODEL), 0.01),
        'norm1_g': 1.0 + nrm(ks[5], (L, D_MODEL), 0.02),
        'w_in': nrm(ks[6], (L, D_MODEL, D_IN_ALL), D_MODEL ** -0.5),
        'conv_w': nrm(ks[7], (L, CONV_K, CONV_WIDTH), CONV_K ** -0.5),
        'q_a_norm_g': 1.0 + nrm(ks[8], (L, Q_LORA), 0.02),
        'w_q_b': nrm(ks[9], (L, Q_LORA, N_HEADS * QK_HEAD), Q_LORA ** -0.5),
        'kv_a_norm_g': 1.0 + nrm(ks[10], (L, KV_LORA), 0.02),
        'w_kv_b': nrm(ks[11], (L, KV_LORA, N_HEADS * (QK_NOPE + V_HEAD)), KV_LORA ** -0.5),
        'q_norm_g': 1.0 + nrm(ks[12], (L, QK_HEAD), 0.02),
        'k_norm_g': 1.0 + nrm(ks[13], (L, QK_HEAD), 0.02),
        'w_o': nrm(ks[14], (L, D_MODEL, D_MODEL), D_MODEL ** -0.5),
        'norm2_g': 1.0 + nrm(ks[15], (L, D_MODEL), 0.02),
        'w_router_group': nrm(ks[16], (L, D_MODEL, N_GROUPS), D_MODEL ** -0.5),
        'b_router_group': nrm(ks[17], (L, N_GROUPS), 0.01),
        'w_router_expert': nrm(ks[18], (L, D_MODEL, N_EXPERTS), D_MODEL ** -0.5),
        'b_router_expert': nrm(ks[19], (L, N_EXPERTS), 0.01),
        'w_exp_gate': nrm(ks[20], (L, N_GROUPS, EXPERTS_PER_GROUP, D_MODEL, D_EXPERT), D_MODEL ** -0.5),
        'w_exp_up': nrm(ks[21], (L, N_GROUPS, EXPERTS_PER_GROUP, D_MODEL, D_EXPERT), D_MODEL ** -0.5),
        'w_exp_down': nrm(ks[22], (L, N_GROUPS, EXPERTS_PER_GROUP, D_EXPERT, D_MODEL), D_EXPERT ** -0.5),
    }

def reference(x, c, positions, w_ada, b_ada, norm1_g, w_in, conv_w, q_a_norm_g, w_q_b, kv_a_norm_g, w_kv_b,
              q_norm_g, k_norm_g, w_o, norm2_g, w_router_group, b_router_group, w_router_expert, b_router_expert,
              w_exp_gate, w_exp_up, w_exp_down):
    cos, sin = rope_tables(positions)
    c_act = jax.nn.silu(c)
    for l in range(DEPTH):
        mod = (c_act @ w_ada[l] + b_ada[l])[:, None, :]
        shift1, scale1, gate1, shift2, scale2, gate2 = jnp.split(mod, 6, axis=-1)

        h = rms_norm(x, norm1_g[l]) * (1.0 + scale1) + shift1
        z = h @ w_in[l]
        zx, zb, zc, q_lat, kv_lat, k_rope_raw, zg_conv, zg_mla = jnp.split(z, COL_SPLITS, axis=-1)
        y_conv = zb * short_causal_conv(zc * zx, conv_w[l])
        y_mla = mla_branch(q_lat, kv_lat, k_rope_raw, cos, sin, q_a_norm_g[l], w_q_b[l], kv_a_norm_g[l],
                           w_kv_b[l], q_norm_g[l], k_norm_g[l])
        merged = jax.nn.sigmoid(zg_conv) * y_conv + jax.nn.sigmoid(zg_mla) * y_mla
        x = x + gate1 * (merged @ w_o[l])

        h2 = rms_norm(x, norm2_g[l]) * (1.0 + scale2) + shift2
        y_moe = hierarchical_moe(h2, w_router_group[l], b_router_group[l], w_router_expert[l], b_router_expert[l],
                                 w_exp_gate[l], w_exp_up[l], w_exp_down[l])
        x = x + gate2 * y_moe
    return x


_drawn_inputs = setup_inputs


def setup_inputs(seed=0):
    import zlib

    import numpy as np

    out = dict(_drawn_inputs(seed))
    spreads = {}
    factors = {'q_a_norm_g': 8.0,
     'kv_a_norm_g': 8.0,
     'q_norm_g': 8.0,
     'k_norm_g': 8.0,
     'b_router_group': 24.895,
     'b_router_expert': 19.973,
     'norm2_g': 4.406}
    for name, (base, spread) in spreads.items():
        noise = np.random.default_rng([zlib.crc32(name.encode()), seed]).standard_normal(out[name].shape)
        drawn = base * np.exp(spread * noise) if base else spread * noise
        out[name] = __import__('jax').numpy.asarray(drawn.astype(out[name].dtype))
    for name, factor in factors.items():
        out[name] = (out[name] * factor).astype(out[name].dtype)
    return out
```

```python
from contextlib import ExitStack

import concourse.bass as bass
from concourse import mybir

F32 = mybir.dt.float32
I32 = mybir.dt.int32
ACT = mybir.ActivationFunctionType
ALU = mybir.AluOpType
AX_X = mybir.AxisListType.X
PI = 3.14159265358979

P = 128
D = 1024
T = 256
KT = D // P
TT = T // P
HEADS = 8
NOPE, ROPE = 128, 64
QK = NOPE + ROPE
QL, KVL = 384, 256
GROUPS, PER_GROUP = 4, 8
EXPERTS = GROUPS * PER_GROUP
FF = 256
SLOTS = 2 * T
NARROW = 64
WIDE = T
EPS = 1e-6
LOW = -1.0e30
CHUNK = 64

SMALL_WIDTHS = (("b_ada", 48), ("g1", KT), ("g2", KT), ("c", KT), ("g_qa", 3), ("g_kva", 2),
                ("gq_nope", 1), ("gk_nope", 1), ("gq_rope", 1), ("gk_rope", 1), ("conv", 3 * KT),
                ("b_router", 36), ("w_router", KT * 36))
CONST_WIDTHS = (("ident", P), ("before", P), ("swap", P), ("slot_no", SLOTS), ("mask", T),
                ("group_no", GROUPS), ("expert_no", PER_GROUP), ("inv_freq", 1))


def places(widths):
    at, out = 0, {}
    for name, width in widths:
        out[name] = (at, width)
        at += width
    return out, at


SMALL, N_SMALL = places(SMALL_WIDTHS)
CONST, N_CONST = places(CONST_WIDTHS)

ADA_ITEMS, ADA_TILES = 12, 4
ADA_COLS = KT * ADA_TILES * P
LAT_TILES = 5
LAT_COLS = KT * (LAT_TILES * P + ROPE)
CONV_COLS = KT * 5 * P
WQ_AT = CONV_COLS
WKV_AT = WQ_AT + 3 * QK
MIX_COLS = WKV_AT + 2 * 256
WO_COLS = KT * 4 * P
GU_COLS = 2 * KT * FF
DOWN_COLS = (FF // P) * D
EX_SLOTS = 4
YW = SLOTS + WIDE


def block_kernel(nc, xT_d, pos_d, small_d, const_d, ada_d, lat_d, mix_d, wo_d, gu_d, down_d, out_d):
    with ExitStack() as ctx:
        def sb(name, shape, dt=F32):
            return ctx.enter_context(nc.sbuf_tensor(name, shape, dt))

        def sem(name):
            return ctx.enter_context(nc.semaphore(name))

        ps = ctx.enter_context(nc.psum_tensor("ps", [P, 8, 512], F32))

        wex = sb("wex", [P, EX_SLOTS, GU_COLS + DOWN_COLS])
        wmix = sb("wmix", [P, 2, MIX_COLS])
        wmix_flat = wmix[:].rearrange("p a b -> p (a b)")
        xg = wmix_flat[:, 0:KT * YW].rearrange("p (k s) -> p k s", k=KT)
        yT = wmix_flat[:, KT * YW:2 * KT * YW].rearrange("p (k s) -> p k s", k=KT)
        xT = sb("xT", [P, KT, T])
        act2 = sb("act2", [P, 2 * KT, T])
        hT = act2[:, 0:KT, :]
        merged = act2[:, KT:2 * KT, :]
        h2_rows = merged.rearrange("p (t a) n -> p t (a n)", t=TT)
        y_rows = act2[:].rearrange("p k n -> p (k n)")
        small = sb("small", [P, N_SMALL])
        const = sb("const", [P, N_CONST])
        ones = sb("ones", [P, P])
        eps_q = sb("eps_q", [P, 1])
        eps_1 = sb("eps_1", [P, 1])
        c_act = sb("c_act", [P, KT])
        mod = sb("mod", [P, 48])
        a12 = sb("a12", [P, 2, KT])
        cos_t = sb("cos_t", [ROPE, T])
        sin_t = sb("sin_t", [ROPE, T])
        k_rot = sb("k_rot", [ROPE, T])
        k_rope_sq = sb("k_rope_sq", [ROPE, T])
        work = sb("work", [P, 7100])
        work_at = [0]

        def piece(cols, parts=P):
            a = work_at[0]
            work_at[0] += cols
            assert work_at[0] <= 7100
            return work[0:parts, a:a + cols]

        q_lat = piece(3 * T).rearrange("p (k n) -> p k n", k=3)
        kv_lat = piece(2 * T).rearrange("p (k n) -> p k n", k=2)
        q_sq = piece(T)
        k_sq = piece(T)
        qr_sq = piece(T, ROPE)
        q_n = piece(T)
        q_x = piece(T, ROPE)
        q_r = piece(T, ROPE)
        rope_t = piece(T, ROPE)
        k_n = piece(T)
        k_r = piece(T, ROPE)
        v_sb = piece(2 * P).rearrange("p (a b) -> p a b", a=2)
        rms = piece(2 * T)
        rk_s, rk = rms[:, 0:T], rms[:, T:2 * T]
        scores = piece(P + T)
        probs = piece(P + T)
        pT = piece(P + T)
        zx = piece(T)
        t_gate = piece(T)
        m_gate = piece(T)
        conv_t = piece(T)
        y_conv = piece(T)
        o_t = zx
        u = piece(T + 2)
        stat = piece(16)
        posi, posf = q_x.bitcast(I32), k_r
        work_at[0] = 0
        sel = piece(TT * SLOTS).rearrange("p (t s) -> p t s", t=TT)
        sel_w = piece(TT * SLOTS).rearrange("p (t s) -> p t s", t=TT)
        comb_t = piece(SLOTS)
        silu_t = sel.rearrange("p t (m n) -> p t m n", m=2)
        act_t = sel_w.rearrange("p t (m n) -> p t m n", m=2)
        comb = piece(4 * T).rearrange("p (s n) -> p s n", s=4)
        lg = piece(72).rearrange("p (t n) -> p t n", t=TT)
        r2s = piece(T)
        r2 = piece(T)
        g_work = piece(5 * 8).rearrange("p (a t n) -> p a t n", a=5, t=TT)
        e_work = piece(6 * 16).rearrange("p (a t n) -> p a t n", a=6, t=TT)
        s_work = piece(24).rearrange("p (a t) -> p a t", a=12)
        oh = piece(4 * 64).rearrange("p (a t n) -> p a t n", a=4, t=TT)
        pos_e = piece(64).rearrange("p (t n) -> p t n", t=TT)
        cnt = piece(EXPERTS)
        incl = piece(EXPERTS)
        offf = piece(EXPERTS)
        table = sb("table", [1, 2 * EXPERTS], I32)

        def sm(name, i=0, n=None, parts=P):
            a, w = SMALL[name]
            return small[0:parts, a + i:a + i + (n or w)]

        def co(name, parts=P):
            a, w = CONST[name]
            return const[0:parts, a:a + w]

        ident, before = co("ident"), co("before")

        x_landed, small_landed, const_landed, pos_landed = sem("x_landed"), sem("small_landed"), sem("const_landed"), sem("pos_landed")
        mix_landed = [sem("mix_landed0"), sem("mix_landed1")]
        ada_done = sem("ada_done")
        gu_landed = [sem(f"gu_landed{s}") for s in range(EX_SLOTS)]
        down_landed = [sem(f"down_landed{s}") for s in range(EX_SLOTS)]
        dve_step = sem("dve_step")
        act_step = sem("act_step")
        setup_done = sem("setup_done")
        c_ready, xsq_ready, xss_ready, r1_ready = sem("c_ready"), sem("xsq_ready"), sem("xss_ready"), sem("r1_ready")
        h_ready = sem("h_ready")
        lat_ready, lat_sq_ready, lat_ss_ready, lat_rms_ready = sem("lat_ready"), sem("lat_sq_ready"), sem("lat_ss_ready"), sem("lat_rms_ready")
        angles_ready, trig_ready = sem("angles_ready"), sem("trig_ready")
        krope_ready, kswap_ready, lat_norm_ready = sem("krope_ready"), sem("kswap_ready"), sem("lat_norm_ready")
        qk_ready, qr_ready, v_ready = sem("qk_ready"), sem("qr_ready"), sem("v_ready")
        sq_ready, v_copied, qx_ready = sem("sq_ready"), sem("v_copied"), sem("qx_ready")
        kss_ready, qss_ready, swap_ready = sem("kss_ready"), sem("qss_ready"), sem("swap_ready")
        rk_sqrt, qs_sqrt, kq_ready = sem("rk_sqrt"), sem("qs_sqrt"), sem("kq_ready")
        zxc_ready, zx_copied, u_done = sem("zxc_ready"), sem("zx_copied"), sem("u_done")
        s_ready, max_ready, exp_done, p_ready = sem("s_ready"), sem("max_ready"), sem("exp_done"), sem("p_ready")
        zbg_ready, conv_gate_ready, y_done = sem("zbg_ready"), sem("conv_gate_ready"), sem("y_done")
        pT_ready, pT_copied = sem("pT_ready"), sem("pT_copied")
        zgm_ready, mla_gate_ready = sem("zgm_ready"), sem("mla_gate_ready")
        o_ready, merged_ready = sem("o_ready"), sem("merged_ready")
        wo_ready, x2_ready, x2sq_ready, x2ss_ready, r2_ready, h2_ready = (sem("wo_ready"), sem("x2_ready"), sem("x2sq_ready"), sem("x2ss_ready"), sem("r2_ready"), sem("h2_ready"))
        lg_ready, h2r_ready, h2r_copied = sem("lg_ready"), sem("h2r_ready"), sem("h2r_copied")
        gdiff_ready, gexp_ready, ediff_ready, eexp_ready = sem("gdiff_ready"), sem("gexp_ready"), sem("ediff_ready"), sem("eexp_ready")
        onehot_ready, rank_ready, table_ready, sel_ready, comb_rows_ready = (sem("onehot_ready"), sem("rank_ready"), sem("table_ready"), sem("sel_ready"), sem("comb_rows_ready"))
        pad_done = sem("pad_done")
        xg_ready, xg_act, xg_dve = sem("xg_ready"), sem("xg_act"), sem("xg_dve")
        comb_ready, comb_copied = sem("comb_ready"), sem("comb_copied")
        gateup_ready, silu_done, act_done, down_ready, y_act, y_dve = (sem("gateup_ready"), sem("silu_done"), sem("act_done"), sem("down_ready"), sem("y_act"), sem("y_dve"))
        yr_ready, yr_copied, out_ready, out_done, out_stored = (sem("yr_ready"), sem("yr_copied"), sem("out_ready"), sem("out_done"), sem("out_stored"))

        MIX0 = 5
        ADA2 = MIX0 + HEADS
        WO0 = ADA2 + 8
        block = ctx.enter_context(nc.Block())

        @block.sync
        def _(sp):
            sp.dma_start(xT[:], xT_d).then_inc(x_landed, 16)
            sp.dma_start(small[:], small_d).then_inc(small_landed, 16)
            sp.dma_start(const[:], const_d).then_inc(const_landed, 16)
            sp.dma_start(posi, pos_d).then_inc(pos_landed, 16)

            def ring(n, dst_cols, src):
                before_it = n - 2
                if 0 <= before_it < 4:
                    sp.wait_ge(ada_done, before_it + 1)
                elif before_it == 4:
                    sp.wait_ge(lat_ready, 1)
                elif MIX0 <= before_it < ADA2:
                    sp.wait_ge(zgm_ready, before_it - MIX0 + 1)
                elif before_it >= ADA2:
                    sp.wait_ge(ada_done, before_it - ADA2 + 5)
                sp.dma_start(wmix[:, n % 2, 0:dst_cols], src).then_inc(mix_landed[n % 2], 16)

            for n in range(4):
                ring(n, ADA_COLS, ada_d[n])
            ring(4, LAT_COLS, lat_d)
            for j in range(HEADS):
                ring(MIX0 + j, MIX_COLS, mix_d[j])
                if 1 <= j <= EX_SLOTS:
                    s = j - 1
                    sp.dma_start(wex[:, s, 0:GU_COLS], gu_d[s]).then_inc(gu_landed[s], 16)
                    sp.dma_start(wex[:, s, GU_COLS:], down_d[s]).then_inc(down_landed[s], 16)
            for n in range(8):
                ring(ADA2 + n, ADA_COLS, ada_d[4 + n])
            for n in range(2):
                ring(WO0 + n, WO_COLS, wo_d[n])
            with sp.Fori(0, EXPERTS // EX_SLOTS - 1) as i:
                for s in range(EX_SLOTS):
                    sp.wait_ge(gateup_ready, i * (2 * EX_SLOTS) + (2 * s + 2))
                    sp.dma_start(wex[:, s, 0:GU_COLS], gu_d[bass.ds(i * EX_SLOTS + (s + EX_SLOTS), 1)].rearrange("a p c -> p (a c)")).then_inc(gu_landed[s], 16)
                    sp.wait_ge(down_ready, i * EX_SLOTS + (s + 1))
                    sp.dma_start(wex[:, s, GU_COLS:], down_d[bass.ds(i * EX_SLOTS + (s + EX_SLOTS), 1)].rearrange("a p c -> p (a c)")).then_inc(down_landed[s], 16)
            for m in range(KT):
                sp.wait_ge(out_done, m + 1)
                sp.dma_start(out_d[m], xT[:, m, :]).then_inc(out_stored, 16)
            sp.wait_ge(out_stored, 16 * KT)

        @block.gpsimd
        def _(pool):
            pool.wait_ge(wo_ready, 2)
            nc.gpsimd.memset(xg[:, :, SLOTS:YW], 0.0).then_inc(pad_done, 1)

        @block.scalar
        def _(act):
            act.wait_ge(small_landed, 16)
            nc.scalar.activation(c_act[:], sm("c"), ACT.Silu).then_inc(c_ready, 1)
            act.wait_ge(x_landed, 16)
            nc.scalar.activation(merged, xT[:], ACT.Square).then_inc(xsq_ready, 1)
            act.wait_ge(angles_ready, 1)
            nc.scalar.activation(sin_t[:], sin_t[:], ACT.Sin)
            nc.scalar.activation(cos_t[:], cos_t[:], ACT.Sin).then_inc(trig_ready, 1)
            act.wait_ge(xss_ready, 1)
            act.wait_ge(setup_done, 4)
            nc.scalar.activation(rms[:, 0:T], ps[:, 3, 0:T], ACT.Sqrt, bias=eps_1[:], scale=1.0 / D).then_inc(r1_ready, 1)

            act.wait_ge(lat_ready, 1)
            nc.scalar.activation(merged[:, 0:2, :], ps[:, 1, :], ACT.Square)
            nc.scalar.activation(merged[:, 2:4, :], ps[:, 2, :], ACT.Square)
            nc.scalar.activation(merged[:, 4, :], ps[:, 4, 0:T], ACT.Square)
            nc.scalar.activation(k_rope_sq[:], ps[0:ROPE, 4, T:2 * T], ACT.Square).then_inc(lat_sq_ready, 1)
            act.wait_ge(lat_ss_ready, 1)
            nc.scalar.activation(rms[:, 0:T], ps[:, 3, 0:T], ACT.Sqrt, bias=eps_1[:], scale=1.0 / QL)
            nc.scalar.activation(rms[:, T:2 * T], ps[:, 3, T:2 * T], ACT.Sqrt, bias=eps_1[:], scale=1.0 / KVL).then_inc(lat_rms_ready, 1)

            with act.Fori(0, HEADS // 2) as i:
                for half in range(2):
                    n = i * 2 + (half + 1)
                    act.wait_ge(qk_ready, n)
                    nc.scalar.activation(q_sq, ps[:, 0, 0:T], ACT.Square)
                    nc.scalar.activation(k_sq, ps[:, 0, T:2 * T], ACT.Square)
                    act.wait_ge(qr_ready, n)
                    nc.scalar.activation(qr_sq, ps[0:ROPE, 1, 0:T], ACT.Square).then_inc(sq_ready, 1)
                    act.wait_ge(v_ready, n)
                    nc.scalar.copy(v_sb, ps[:, 2, 0:2 * P].rearrange("p (a b) -> p a b", a=2)).then_inc(v_copied, 1)
                    act.wait_ge(kss_ready, n)
                    nc.scalar.activation(rk_s, ps[:, 3, 0:T], ACT.Sqrt, bias=eps_1[:], scale=1.0 / QK).then_inc(rk_sqrt, 1)
                    act.wait_ge(qss_ready, n)
                    nc.scalar.activation(stat[:, 0:2], ps[:, 4, 0:2], ACT.Sqrt, bias=eps_q[:], scale=1.0).then_inc(qs_sqrt, 1)
                    act.wait_ge(zxc_ready, n)
                    nc.scalar.copy(zx, ps[:, 5, 0:T]).then_inc(zx_copied, 1)
                    act.wait_ge(max_ready, n + 1)
                    nc.scalar.activation(probs[:, 0:P], scores[:, 0:P], ACT.Exp, bias=stat[:, 6:7], scale=stat[:, 2:3], accum_out=stat[:, 8:9])
                    nc.scalar.activation(probs[:, P:P + T], scores[:, P:P + T], ACT.Exp, bias=stat[:, 7:8], scale=stat[:, 3:4], accum_out=stat[:, 9:10]).then_inc(exp_done, 1)
                    act.wait_ge(zbg_ready, n)
                    nc.scalar.activation(t_gate, ps[:, 6, T:2 * T], ACT.Tanh, scale=0.5).then_inc(conv_gate_ready, 1)
                    act.wait_ge(pT_ready, n)
                    nc.scalar.copy(pT, ps[:, 4, 0:P + T]).then_inc(pT_copied, 1)
                    act.wait_ge(zgm_ready, n)
                    nc.scalar.activation(m_gate, ps[:, 7, 0:T], ACT.Tanh, scale=0.5).then_inc(mla_gate_ready, 1)

            for a in range(2):
                act.wait_ge(x2_ready, a + 1)
                act.wait_ge(wo_ready, 2)
                nc.scalar.activation(hT[:, 4 * a:4 * a + 4, :], xT[:, 4 * a:4 * a + 4, :], ACT.Square).then_inc(x2sq_ready, 1)
            act.wait_ge(x2ss_ready, 1)
            nc.scalar.activation(r2s, ps[:, 5, 0:T], ACT.Sqrt, bias=eps_1[:], scale=1.0 / D).then_inc(r2_ready, 1)
            for b in range(4):
                act.wait_ge(h2r_ready, b + 1)
                nc.scalar.copy(h2_rows[:, b // 2, (b % 2) * 512:(b % 2) * 512 + 512], ps[:, 1 + b, :]).then_inc(h2r_copied, 1)
                if b == 1:
                    act.wait_ge(gdiff_ready, 1)
                    nc.scalar.activation(g_work[:, 1], g_work[:, 1], ACT.Exp).then_inc(gexp_ready, 1)
            act.wait_ge(ediff_ready, 1)
            nc.scalar.activation(s_work[:, 6, :], s_work[:, 5, :], ACT.Exp).then_inc(eexp_ready, 1)
            for k in range(0, KT, 2):
                act.wait_ge(xg_ready, k + 1)
                nc.scalar.copy(xg[:, k, 0:SLOTS], ps[:, k, :]).then_inc(xg_act, 1)
            act.wait_ge(comb_ready, 1)
            nc.scalar.copy(comb, ps[:, 2:4, :].rearrange("p b (s n) -> p (b s) n", s=2)).then_inc(comb_copied, 1)

            act.wait_ge(table_ready, 1)
            act.sem_inc(y_act, 1)
            with act.Fori(0, EXPERTS // 2) as i:
                for par in range(2):
                    n = i * 2 + (par + 1)
                    off = act.value_load(table[0:1, bass.ds(i * 2 + par, 1)], min_val=0, max_val=SLOTS)
                    for f in range(2):
                        act.wait_ge(gateup_ready, i * 4 + (2 * par + f + 1))
                        nc.scalar.activation(silu_t[:, par, f, :], ps[:, 2 * par + f, 0:T], ACT.Silu).then_inc(silu_done, 1)
                    act.wait_ge(down_ready, n)
                    nc.scalar.copy(yT[:, 0:4, bass.ds(off, WIDE)], ps[:, 4:6, :].rearrange("p b (s n) -> p (b s) n", s=2)).then_inc(y_act, 1)
            for m in range(KT):
                act.wait_ge(yr_ready, m + 1)
                nc.scalar.copy(y_rows[:, (m % 2) * 512:(m % 2) * 512 + 512], ps[:, m % 2, :]).then_inc(yr_copied, 1)

        @block.tensor
        def _(pe):
            def mm(out, lhsT, rhs, start, stop, **kw):
                return nc.tensor.matmul(out, lhsT, rhs, start=start, stop=stop, **kw)

            pe.wait_ge(setup_done, 4)
            pe.wait_ge(xsq_ready, 1)
            for k in range(KT):
                last = mm(ps[:, 3, 0:T], ones[:], merged[:, k, :], k == 0, k == KT - 1)
            last.then_inc(xss_ready, 1)

            def ada_item(slot, first_col):
                w = wmix[:, slot, 0:ADA_COLS].rearrange("p (m k c) -> p m k c", m=ADA_TILES, k=KT)
                for m in range(ADA_TILES):
                    for k in range(KT):
                        last = mm(ps[:, 0, bass.ds(first_col + m, 1)], w[:, m, k, :], c_act[:, k:k + 1], k == 0, k == KT - 1)
                return last

            pe.wait_ge(c_ready, 1)
            with pe.Fori(0, 2) as i:
                for a in range(2):
                    pe.wait_ge(mix_landed[a], i * 16 + 16)
                    ada_item(a, i * 8 + 4 * a).then_inc(ada_done, 1)

            pe.wait_ge(mix_landed[0], 16 * 3)
            pe.wait_ge(h_ready, KT)
            w = wmix[:, 0, 0:KT * LAT_TILES * P].rearrange("p (m k c) -> p m k c", m=LAT_TILES, k=KT)
            wr = wmix[:, 0, KT * LAT_TILES * P:LAT_COLS].rearrange("p (k c) -> p k c", k=KT)
            lat_ps = [ps[:, 1, 0:T], ps[:, 1, T:2 * T], ps[:, 2, 0:T], ps[:, 2, T:2 * T], ps[:, 4, 0:T]]
            for m in range(LAT_TILES):
                for k in range(KT):
                    mm(lat_ps[m], w[:, m, k, :], hT[:, k, :], k == 0, k == KT - 1)
            for k in range(KT):
                last = mm(ps[0:ROPE, 4, T:2 * T], wr[:, k, :], hT[:, k, :], k == 0, k == KT - 1)
            last.then_inc(lat_ready, 1)
            pe.wait_ge(lat_sq_ready, 1)
            for k in range(3):
                mm(ps[:, 3, 0:T], ones[:], merged[:, k, :], k == 0, k == 2)
            for k in range(2):
                last = mm(ps[:, 3, T:2 * T], ones[:], merged[:, 3 + k, :], k == 0, k == 1)
            last.then_inc(lat_ss_ready, 1)
            pe.wait_ge(krope_ready, 1)
            mm(ps[:, 5, 0:T], co("swap", ROPE), k_r, True, True).then_inc(kswap_ready, 1)
            pe.wait_ge(lat_norm_ready, 1)

            with pe.Fori(0, HEADS // 2) as i:
                for half in range(2):
                    done = i * 2 + half
                    slot = (MIX0 + half) % 2
                    w = wmix[:, slot, 0:CONV_COLS].rearrange("p (m k c) -> p m k c", m=5, k=KT)
                    wq = wmix[:, slot, WQ_AT:WKV_AT].rearrange("p (k c) -> p k c", k=3)
                    wkv = wmix[:, slot, WKV_AT:MIX_COLS].rearrange("p (k c) -> p k c", k=2)

                    def conv_tile(m, out):
                        for k in range(KT):
                            last = mm(out, w[:, m, k, :], hT[:, k, :], k == 0, k == KT - 1)
                        return last

                    pe.wait_ge(mix_landed[slot], i * 16 + 16 * ((MIX0 + half) // 2 + 1))
                    pe.wait_ge(kq_ready, done + 1)
                    for k in range(3):
                        mm(ps[:, 0, 0:T], wq[:, k, 0:NOPE], q_lat[:, k, :], k == 0, k == 2)
                    for k in range(2):
                        last = mm(ps[:, 0, T:2 * T], wkv[:, k, 0:NOPE], kv_lat[:, k, :], k == 0, k == 1)
                    last.then_inc(qk_ready, 1)
                    for k in range(3):
                        last = mm(ps[0:ROPE, 1, 0:T], wq[:, k, NOPE:QK], q_lat[:, k, :], k == 0, k == 2)
                    last.then_inc(qr_ready, 1)
                    pe.wait_ge(merged_ready, done + 1)
                    for t in range(TT):
                        for k in range(2):
                            last = mm(ps[:, 2, t * P:(t + 1) * P], kv_lat[:, k, t * P:(t + 1) * P], wkv[:, k, NOPE:], k == 0, k == 1)
                    last.then_inc(v_ready, 1)
                    pe.wait_ge(u_done, done + 1)
                    conv_tile(0, ps[:, 5, 0:T])
                    pe.wait_ge(sq_ready, done + 1)
                    pe.wait_ge(max_ready, done + 1)
                    mm(ps[:, 3, 0:T], ones[:], k_sq, True, False)
                    mm(ps[:, 3, 0:T], ones[0:ROPE, :], k_rope_sq[:], False, True).then_inc(kss_ready, 1)
                    for t in range(TT):
                        mm(ps[:, 4, t:t + 1], q_sq[:, t * P:(t + 1) * P], ones[:, 0:1], True, False)
                        last = mm(ps[:, 4, t:t + 1], qr_sq[:, t * P:(t + 1) * P], ones[0:ROPE, 0:1], False, True)
                    last.then_inc(qss_ready, 1)
                    pe.wait_ge(qx_ready, done + 1)
                    mm(ps[:, 1, T:2 * T], co("swap", ROPE), q_x, True, True).then_inc(swap_ready, 1)
                    conv_tile(1, ps[:, 5, T:2 * T]).then_inc(zxc_ready, 1)
                    pe.wait_ge(kq_ready, done + 2)
                    pe.wait_ge(rk_sqrt, done + 1)
                    mm(ps[:, 3, 0:P], q_n[:, 0:P], k_n[:, 0:P], True, False)
                    mm(ps[:, 3, 0:P], q_r[:, 0:P], k_r[:, 0:P], False, True)
                    mm(ps[:, 3, P:P + T], q_n[:, P:T], k_n, True, False)
                    mm(ps[:, 3, P:P + T], q_r[:, P:T], k_r, False, True).then_inc(s_ready, 1)
                    pe.wait_ge(y_done, done + 1)
                    conv_tile(2, ps[:, 6, 0:T])
                    conv_tile(3, ps[:, 6, T:2 * T]).then_inc(zbg_ready, 1)
                    pe.wait_ge(p_ready, done + 1)
                    nc.tensor.transpose(ps[:, 4, 0:P], probs[:, 0:P], ident)
                    nc.tensor.transpose(ps[:, 4, P:2 * P], probs[:, P:2 * P], ident)
                    nc.tensor.transpose(ps[:, 4, 2 * P:3 * P], probs[:, 2 * P:3 * P], ident).then_inc(pT_ready, 1)
                    conv_tile(4, ps[:, 7, 0:T]).then_inc(zgm_ready, 1)
                    pe.wait_ge(pT_copied, done + 1)
                    mm(ps[:, 2, T:2 * T], v_sb[:, 0, :], pT[:, 0:T], True, False)
                    mm(ps[:, 2, T + P:2 * T], v_sb[:, 1, :], pT[:, T:T + P], False, True).then_inc(o_ready, 1)

            with pe.Fori(0, 4) as i:
                for a in range(2):
                    slot = (ADA2 + a) % 2
                    pe.wait_ge(mix_landed[slot], i * 16 + 16 * ((ADA2 + a) // 2 + 1))
                    ada_item(slot, i * 8 + (16 + 4 * a)).then_inc(ada_done, 1)

            pe.wait_ge(merged_ready, HEADS + 1)
            for a in range(2):
                slot = (WO0 + a) % 2
                pe.wait_ge(mix_landed[slot], 16 * ((WO0 + a) // 2 + 1))
                w = wmix[:, slot, 0:WO_COLS].rearrange("p (m k c) -> p m k c", m=4, k=KT)
                for m in range(4):
                    for k in range(KT):
                        last = mm(ps[:, 1 + 2 * a + m // 2, (m % 2) * T:(m % 2 + 1) * T], w[:, m, k, :], merged[:, k, :], k == 0, k == KT - 1)
                last.then_inc(wo_ready, 1)
            for k in range(KT):
                if k % 4 == 0:
                    pe.wait_ge(x2sq_ready, k // 4 + 1)
                last = mm(ps[:, 5, 0:T], ones[:], hT[:, k, :], k == 0, k == KT - 1)
            last.then_inc(x2ss_ready, 1)

            pe.wait_ge(h2_ready, KT)
            a0 = SMALL["w_router"][0]
            for t in range(TT):
                for k in range(KT):
                    last = mm(ps[:, 6, 64 * t:64 * t + 36], hT[:, k, t * P:(t + 1) * P], small[:, a0 + 36 * k:a0 + 36 * k + 36], k == 0, k == KT - 1)
            last.then_inc(lg_ready, 1)
            for b in range(4):
                for q in range(4):
                    last = nc.tensor.transpose(ps[:, 1 + b, q * P:(q + 1) * P], hT[:, (b % 2) * 4 + q, (b // 2) * P:(b // 2 + 1) * P], ident)
                last.then_inc(h2r_ready, 1)
            pe.wait_ge(onehot_ready, 1)
            mm(ps[:, 7, 0:32], before, oh[:, 2, 0, :], True, True)
            mm(ps[:, 7, 32:64], ones[:], oh[:, 2, 0, :], True, False)
            mm(ps[:, 7, 32:64], before, oh[:, 2, 1, :], False, True)
            mm(ps[:, 7, 64:96], ones[:], oh[:, 2, 0, :], True, False)
            mm(ps[:, 7, 64:96], ones[:], oh[:, 2, 1, :], False, True).then_inc(rank_ready, 1)
            pe.wait_ge(h2r_copied, 4)
            pe.wait_ge(sel_ready, 2)
            for k in range(KT):
                for t in range(TT):
                    last = mm(ps[:, k, :], h2_rows[:, t, k * P:(k + 1) * P], sel[:, t, :], t == 0, t == TT - 1)
                last.then_inc(xg_ready, 1)
            pe.wait_ge(comb_rows_ready, 2)
            pe.wait_ge(xg_act, 2)
            pe.wait_ge(xg_dve, 2)
            for s in range(4):
                for t in range(TT):
                    c0 = (s % 2) * T + t * P
                    last = nc.tensor.transpose(ps[:, 2 + s // 2, c0:c0 + P], sel_w[:, t, s * P:(s + 1) * P], ident)
            last.then_inc(comb_ready, 1)

            pe.wait_ge(xg_act, 4)
            pe.wait_ge(xg_dve, 4)
            pe.wait_ge(pad_done, 1)
            pe.wait_ge(comb_copied, 1)
            pe.wait_ge(table_ready, 1)

            def gate_up(slot, par, off, width):
                w = wex[:, slot, 0:GU_COLS].rearrange("p (g k c) -> p g k c", g=2, k=KT)
                for f in range(2):
                    for g in range(2):
                        for k in range(KT):
                            last = mm(ps[:, 2 * par + f, g * T:g * T + width], w[:, g, k, f * P:(f + 1) * P], xg[:, k, bass.ds(off, width)], k == 0, k == KT - 1)
                    last.then_inc(gateup_ready, 1)

            def down(slot, par, f, width):
                w = wex[:, slot, GU_COLS:].rearrange("p (f c) -> p f c", f=2)
                for m in range(KT):
                    last = mm(ps[:, 4 + m // 2, (m % 2) * T:(m % 2) * T + width], w[:, f, m * P:(m + 1) * P], act_t[:, par, f, 0:width], f == 0 and m % 2 == 0, f == 1, skip_group_check=True)
                return last

            with pe.Fori(0, EXPERTS // EX_SLOTS) as i:
                for s in range(EX_SLOTS):
                    par = s % 2
                    off = pe.value_load(table[0:1, bass.ds(i * EX_SLOTS + s, 1)], min_val=0, max_val=SLOTS)
                    many = pe.value_load(table[0:1, bass.ds(i * EX_SLOTS + (s + EXPERTS), 1)], min_val=0, max_val=T)
                    pe.wait_ge(gu_landed[s], i * 16 + 16)
                    pe.wait_ge(act_done, i * 8 + (2 * s + 1))
                    with pe.If(many > NARROW):
                        gate_up(s, par, off, WIDE)
                    with pe.Else():
                        gate_up(s, par, off, NARROW)
                    pe.wait_ge(down_landed[s], i * 16 + 16)
                    pe.wait_ge(y_act, i * EX_SLOTS + (s + 1))
                    pe.wait_ge(y_dve, i * EX_SLOTS + (s + 1))
                    pe.wait_ge(act_done, i * 8 + (2 * s + 2))
                    with pe.If(many > NARROW):
                        down(s, par, 0, WIDE)
                        pe.wait_ge(act_done, i * 8 + (2 * s + 3))
                        down(s, par, 1, WIDE).then_inc(down_ready, 1)
                    with pe.Else():
                        down(s, par, 0, NARROW)
                        pe.wait_ge(act_done, i * 8 + (2 * s + 3))
                        down(s, par, 1, NARROW).then_inc(down_ready, 1)

            pe.wait_ge(y_act, EXPERTS + 1)
            pe.wait_ge(y_dve, EXPERTS + 1)

            def turn(m):
                if m >= 2:
                    pe.wait_ge(yr_copied, m - 1)
                for t in range(4):
                    last = nc.tensor.transpose(ps[:, m % 2, t * P:(t + 1) * P], yT[:, m, t * P:(t + 1) * P], ident)
                last.then_inc(yr_ready, 1)

            turn(0)
            for m in range(KT):
                if m + 1 < KT:
                    turn(m + 1)
                pe.wait_ge(yr_copied, m + 1)
                if m >= 4:
                    pe.wait_ge(out_done, m - 3)
                for t in range(4):
                    c0 = (m % 2) * 512 + t * P
                    last = mm(ps[:, 4 + m % 4, 0:T], y_rows[:, c0:c0 + P], comb[:, t, :], t == 0, t == 3)
                last.then_inc(out_ready, 1)

        @block.vector
        def _(dve):
            v = nc.vector
            chain = [0, None]

            def step_value(k):
                return k if chain[1] is None else chain[1] + k

            def link(ins):
                chain[0] += 1
                ins.then_inc(dve_step, 1)
                dve.wait_ge(dve_step, step_value(chain[0]))

            v.memset(ones[:], 1.0).then_inc(setup_done, 1)
            v.memset(eps_1[:], EPS).then_inc(setup_done, 1)
            v.memset(eps_q[:], EPS * QK).then_inc(setup_done, 1)
            v.memset(u, 0.0).then_inc(setup_done, 1)

            C1 = 6.28125
            C2 = 0.0019350051879882812
            C3 = 2 * 3.141592653589793 - C1 - C2
            MAGIC = 1.5 * 2.0 ** 23
            dve.wait_ge(pos_landed, 16)
            dve.wait_ge(const_landed, 16)
            link(v.tensor_copy(posf, posi))
            link(v.tensor_scalar(posf, posf, co("inv_freq", ROPE), None, ALU.mult))
            for out, quarter in ((sin_t, 0.0), (cos_t, 0.25)):
                link(v.tensor_scalar(out[:], posf, 1.0 / (2 * PI), quarter, ALU.mult, ALU.add))
                link(v.tensor_scalar(out[:], out[:], MAGIC, None, ALU.add))
                link(v.tensor_scalar(out[:], out[:], MAGIC, None, ALU.subtract))
                link(v.scalar_tensor_tensor(rope_t, out[:], -C1, posf, ALU.mult, ALU.add))
                link(v.scalar_tensor_tensor(rope_t, out[:], -C2, rope_t, ALU.mult, ALU.add))
                link(v.scalar_tensor_tensor(rope_t, out[:], -C3, rope_t, ALU.mult, ALU.add))
                link(v.tensor_scalar(rope_t, rope_t, 2 * PI * quarter, None, ALU.add))
                last = v.tensor_scalar(out[:], rope_t, 3.141592, -3.141592, ALU.min, ALU.max)
                if quarter:
                    last.then_inc(angles_ready, 1)
                else:
                    link(last)

            dve.wait_ge(x_landed, 16)
            dve.wait_ge(r1_ready, 1)
            link(v.reciprocal(rms[:, T:2 * T], rms[:, 0:T]))
            link(v.tensor_tensor(hT, xT[:], rms[:, T:2 * T].unsqueeze(1).broadcast_to([P, KT, T]), ALU.mult))
            dve.wait_ge(small_landed, 16)
            dve.wait_ge(ada_done, 4)
            link(v.tensor_tensor(mod[:, 0:16], ps[:, 0, 0:16], sm("b_ada", 0, 16), ALU.add))
            link(v.scalar_tensor_tensor(a12[:, 0, :], mod[:, 8:16], 1.0, sm("g1"), ALU.add, ALU.mult))
            for k in range(KT):
                v.tensor_scalar(hT[:, k, :], hT[:, k, :], a12[:, 0, k:k + 1], mod[:, k:k + 1], ALU.mult, ALU.add).then_inc(h_ready, 1)

            dve.wait_ge(lat_sq_ready, 1)
            v.tensor_scalar(k_r, ps[0:ROPE, 4, T:2 * T], sm("gk_rope", parts=ROPE), None, ALU.mult).then_inc(krope_ready, 1)
            dve.wait_ge(lat_rms_ready, 1)
            link(v.reciprocal(rms, rms))
            lat_ps = [ps[:, 1, 0:T], ps[:, 1, T:2 * T], ps[:, 2, 0:T], ps[:, 2, T:2 * T], ps[:, 4, 0:T]]
            for m in range(3):
                link(v.scalar_tensor_tensor(q_lat[:, m, :], lat_ps[m], sm("g_qa", m, 1), rms[:, 0:T], ALU.mult, ALU.mult))
            for m in range(2):
                link(v.scalar_tensor_tensor(kv_lat[:, m, :], lat_ps[3 + m], sm("g_kva", m, 1), rms[:, T:2 * T], ALU.mult, ALU.mult))
            dve.wait_ge(trig_ready, 1)
            dve.wait_ge(kswap_ready, 1)
            link(v.tensor_tensor(rope_t, ps[0:ROPE, 5, 0:T], sin_t[:], ALU.mult))
            link(v.tensor_tensor(k_rot[:], k_r, cos_t[:], ALU.mult))
            link(v.tensor_tensor(k_rot[:], k_rot[:], rope_t, ALU.add))
            v.tensor_tensor(stat[:, 15:16], sm("gq_nope"), sm("gk_nope"), ALU.mult).then_inc(lat_norm_ready, 1)

            for read_out in (kq_ready, merged_ready, u_done, max_ready, y_done):
                dve.sem_inc(read_out, 1)
            base, STEPS = chain[0], 14
            with dve.Fori(0, HEADS // 2) as i:
                for half in range(2):
                    n = i * 2 + (half + 1)
                    j = i * 2 + half
                    chain[0], chain[1] = base + half * STEPS, i * (2 * STEPS)
                    dve.wait_ge(sq_ready, n)
                    if half == 0:
                        dve.wait_ge(lat_norm_ready, 1)
                    v.tensor_scalar(q_x, ps[0:ROPE, 1, 0:T], sm("gq_rope", parts=ROPE), None, ALU.mult).then_inc(qx_ready, 1)
                    link(v.tensor_scalar(q_n, ps[:, 0, 0:T], stat[:, 15:16], None, ALU.mult))
                    dve.wait_ge(rk_sqrt, n)
                    link(v.reciprocal(rk, rk_s))
                    link(v.tensor_tensor(k_n, rk, ps[:, 0, T:2 * T], ALU.mult))
                    link(v.tensor_tensor(k_r, k_rot[:], rk[0:ROPE, :], ALU.mult))
                    dve.wait_ge(qx_ready, n)
                    link(v.tensor_tensor(q_r, q_x, cos_t[:], ALU.mult))
                    dve.wait_ge(swap_ready, n)
                    link(v.tensor_tensor(rope_t, sin_t[:], ps[0:ROPE, 1, T:2 * T], ALU.mult))
                    v.tensor_tensor(q_r, q_r, rope_t, ALU.add).then_inc(kq_ready, 1)
                    dve.wait_ge(zx_copied, n)
                    v.tensor_tensor(u[:, 2:T + 2], zx, ps[:, 5, T:2 * T], ALU.mult).then_inc(u_done, 1)
                    dve.wait_ge(u_done, n + 1)
                    c0 = SMALL["conv"][0]
                    link(v.tensor_scalar(conv_t, u[:, 0:T], small[:, bass.ds(j + c0, 1)], None, ALU.mult))
                    link(v.scalar_tensor_tensor(conv_t, u[:, 1:T + 1], small[:, bass.ds(j + (c0 + KT), 1)], conv_t, ALU.mult, ALU.add))
                    link(v.scalar_tensor_tensor(conv_t, u[:, 2:T + 2], small[:, bass.ds(j + (c0 + 2 * KT), 1)], conv_t, ALU.mult, ALU.add))
                    dve.wait_ge(qs_sqrt, n)
                    dve.wait_ge(s_ready, n)
                    v.reciprocal(stat[:, 2:4], stat[:, 0:2])
                    mask = co("mask")
                    v.tensor_tensor_reduce(out=scores[:, 0:P], in0=ps[:, 3, 0:P], in1=mask[:, P:T], scale=1.0, scalar=2 * LOW,
                                           op0=ALU.add, op1=ALU.max, accum_out=stat[:, 4:5])
                    link(v.tensor_tensor_reduce(out=scores[:, P:P + T], in0=ps[:, 3, P:P + T], in1=mask, scale=1.0, scalar=2 * LOW,
                                                op0=ALU.add, op1=ALU.max, accum_out=stat[:, 5:6]))
                    v.scalar_tensor_tensor(stat[:, 6:8], stat[:, 4:6], -1.0, stat[:, 2:4], ALU.mult, ALU.mult).then_inc(max_ready, 1)
                    dve.wait_ge(exp_done, n)
                    link(v.reciprocal(stat[:, 10:12], stat[:, 8:10]))
                    link(v.tensor_scalar(probs[:, 0:P], probs[:, 0:P], stat[:, 10:11], None, ALU.mult))
                    v.tensor_scalar(probs[:, P:P + T], probs[:, P:P + T], stat[:, 11:12], None, ALU.mult).then_inc(p_ready, 1)
                    dve.wait_ge(conv_gate_ready, n)
                    link(v.scalar_tensor_tensor(y_conv, ps[:, 6, 0:T], 0.5, conv_t, ALU.mult, ALU.mult))
                    v.scalar_tensor_tensor(y_conv, t_gate, 1.0, y_conv, ALU.add, ALU.mult).then_inc(y_done, 1)
                    dve.wait_ge(mla_gate_ready, n)
                    dve.wait_ge(o_ready, n)
                    dve.wait_ge(y_done, n + 1)
                    link(v.scalar_tensor_tensor(o_t, m_gate, 1.0, ps[:, 2, T:2 * T], ALU.add, ALU.mult))
                    v.scalar_tensor_tensor(merged[:, bass.ds(j, 1), :].rearrange("p a n -> p (a n)"), o_t, 0.5, y_conv, ALU.mult, ALU.add).then_inc(merged_ready, 1)
                    used = chain[0] - (base + half * STEPS)
                    assert used == STEPS, used
            chain[0], chain[1] = base + HEADS * STEPS, None

            dve.wait_ge(ada_done, ADA_ITEMS)
            link(v.tensor_tensor(mod[:, 16:48], ps[:, 0, 16:48], sm("b_ada", 16, 32), ALU.add))
            link(v.scalar_tensor_tensor(a12[:, 1, :], mod[:, 32:40], 1.0, sm("g2"), ALU.add, ALU.mult))
            for a in range(2):
                dve.wait_ge(wo_ready, a + 1)
                for m in range(4):
                    last = v.scalar_tensor_tensor(xT[:, 4 * a + m, :], ps[:, 1 + 2 * a + m // 2, (m % 2) * T:(m % 2 + 1) * T],
                                                  mod[:, 16 + 4 * a + m:17 + 4 * a + m], xT[:, 4 * a + m, :], ALU.mult, ALU.add)
                last.then_inc(x2_ready, 1)
            dve.wait_ge(x2_ready, 2)
            dve.wait_ge(r2_ready, 1)
            link(v.reciprocal(r2, r2s))
            link(v.tensor_tensor(hT, xT[:], r2.unsqueeze(1).broadcast_to([P, KT, T]), ALU.mult))
            for k in range(KT):
                v.tensor_scalar(hT[:, k, :], hT[:, k, :], a12[:, 1, k:k + 1], mod[:, 24 + k:25 + k], ALU.mult, ALU.add).then_inc(h2_ready, 1)

            dve.wait_ge(lg_ready, 1)
            logits_ps = ps[:, 6, 0:128].rearrange("p (t n) -> p t n", t=TT)[:, :, 0:36]
            link(v.tensor_tensor(lg, logits_ps, sm("b_router").unsqueeze(1).broadcast_to([P, TT, 36]), ALU.add))
            G = [P, TT, GROUPS]
            E = [P, TT, PER_GROUP]
            G4 = [P, GROUPS, PER_GROUP]

            def b(ap, shape):
                return ap.unsqueeze(2).broadcast_to(shape)

            def first_of_max(values, number, top, tmp, onehot, shape, idx):
                link(v.tensor_reduce(top, values, AX_X, ALU.max))
                link(v.tensor_tensor(tmp, values, b(top, shape), ALU.is_equal))
                link(v.tensor_tensor(tmp, tmp, number, ALU.mult))
                link(v.tensor_reduce(idx, tmp, AX_X, ALU.min))
                link(v.tensor_tensor(onehot, number, b(idx, shape), ALU.is_equal))

            g_no = co("group_no").unsqueeze(1).broadcast_to(G)
            e_no = co("expert_no").unsqueeze(1).broadcast_to(E)
            lg_g = lg[:, :, 0:GROUPS]
            first_of_max(lg_g, g_no, s_work[:, 0, :], g_work[:, 0], g_work[:, 2], G, s_work[:, 1, :])
            v.tensor_tensor(g_work[:, 1], lg_g, b(s_work[:, 0, :], G), ALU.subtract).then_inc(gdiff_ready, 1)
            for t in range(TT):
                link(v.tensor_tensor(oh[:, 3, t, :].rearrange("p (g e) -> p g e", g=GROUPS),
                                     lg[:, t, GROUPS:].rearrange("p (g e) -> p g e", g=GROUPS),
                                     g_work[:, 2, t, :].unsqueeze(2).broadcast_to(G4), ALU.mult))
                link(v.tensor_reduce(e_work[:, 0, t, :], oh[:, 3, t, :].rearrange("p (g e) -> p e g", g=GROUPS), AX_X, ALU.add))
            first_of_max(e_work[:, 0], e_no, s_work[:, 2, :], e_work[:, 1], e_work[:, 2], E, s_work[:, 3, :])
            link(v.scalar_tensor_tensor(e_work[:, 3].rearrange("p t n -> p (t n)"), e_work[:, 2].rearrange("p t n -> p (t n)"), LOW,
                                        e_work[:, 0].rearrange("p t n -> p (t n)"), ALU.mult, ALU.add))
            first_of_max(e_work[:, 3], e_no, s_work[:, 4, :], e_work[:, 1], e_work[:, 4], E, s_work[:, 3, :])
            v.tensor_tensor(s_work[:, 5, :], s_work[:, 4, :], s_work[:, 2, :], ALU.subtract).then_inc(ediff_ready, 1)
            for c, e in ((0, 2), (1, 4)):
                for t in range(TT):
                    link(v.tensor_tensor(oh[:, c, t, :].rearrange("p (g e) -> p g e", g=GROUPS),
                                         g_work[:, 2, t, :].unsqueeze(2).broadcast_to(G4),
                                         e_work[:, e, t, :].unsqueeze(1).broadcast_to(G4), ALU.mult))
            v.tensor_tensor(oh[:, 2], oh[:, 0], oh[:, 1], ALU.add).then_inc(onehot_ready, 1)
            dve.wait_ge(gexp_ready, 1)
            link(v.tensor_reduce(s_work[:, 7, :], g_work[:, 1], AX_X, ALU.add))
            dve.wait_ge(eexp_ready, 1)
            link(v.scalar_tensor_tensor(s_work[:, 8, :], s_work[:, 6, :], 1.0, s_work[:, 7, :], ALU.add, ALU.mult))
            link(v.reciprocal(s_work[:, 8, :], s_work[:, 8, :]))
            link(v.tensor_tensor(s_work[:, 9, :], s_work[:, 8, :], s_work[:, 6, :], ALU.mult))
            dve.wait_ge(rank_ready, 1)
            link(v.tensor_copy(cnt, ps[:, 7, 64:96]))
            link(v.tensor_tensor_scan(incl, ones[:, 0:EXPERTS], cnt, 0.0, ALU.mult, ALU.add))
            link(v.tensor_tensor(offf, incl, cnt, ALU.subtract))
            v.tensor_copy(table[0:1, 0:EXPERTS], offf[0:1, :])
            v.tensor_copy(table[0:1, EXPERTS:], cnt[0:1, :]).then_inc(table_ready, 1)
            link(v.tensor_tensor(pos_e, ps[:, 7, 0:64].rearrange("p (t n) -> p t n", t=TT), offf.unsqueeze(1).broadcast_to([P, TT, EXPERTS]), ALU.add))
            for c in range(2):
                link(v.tensor_tensor(oh[:, 3], oh[:, c], pos_e, ALU.mult))
                link(v.tensor_reduce(s_work[:, 10 + c, :], oh[:, 3], AX_X, ALU.add))
            slot_no = co("slot_no")
            for t in range(TT):
                link(v.tensor_scalar(sel[:, t, :], slot_no, s_work[:, 10, t:t + 1], None, ALU.is_equal))
                v.scalar_tensor_tensor(sel[:, t, :], slot_no, s_work[:, 11, t:t + 1], sel[:, t, :], ALU.is_equal, ALU.add).then_inc(sel_ready, 1)
            for t in range(TT):
                link(v.tensor_scalar(sel_w[:, t, :], slot_no, s_work[:, 10, t:t + 1], s_work[:, 8, t:t + 1], ALU.is_equal, ALU.mult))
                link(v.tensor_scalar(comb_t, slot_no, s_work[:, 11, t:t + 1], s_work[:, 9, t:t + 1], ALU.is_equal, ALU.mult))
                v.tensor_tensor(sel_w[:, t, :], sel_w[:, t, :], comb_t, ALU.add).then_inc(comb_rows_ready, 1)
            for k in range(1, KT, 2):
                dve.wait_ge(xg_ready, k + 1)
                v.tensor_copy(xg[:, k, 0:SLOTS], ps[:, k, :]).then_inc(xg_dve, 1)

            dve.wait_ge(table_ready, 1)
            dve.sem_inc(y_dve, 1)
            dve.sem_inc(act_done, 1)
            with dve.Fori(0, EXPERTS // 2) as i:
                for par in range(2):
                    n = i * 2 + (par + 1)
                    off = dve.value_load(table[0:1, bass.ds(i * 2 + par, 1)], min_val=0, max_val=SLOTS)
                    for f in range(2):
                        dve.wait_ge(silu_done, i * 4 + (2 * par + f + 1))
                        v.tensor_tensor(act_t[:, par, f, :], silu_t[:, par, f, :], ps[:, 2 * par + f, T:2 * T], ALU.mult).then_inc(act_done, 1)
                    dve.wait_ge(down_ready, n)
                    v.tensor_copy(yT[:, 4:8, bass.ds(off, WIDE)], ps[:, 6:8, :].rearrange("p b (s n) -> p (b s) n", s=2)).then_inc(y_dve, 1)
            for m in range(KT):
                dve.wait_ge(out_ready, m + 1)
                v.scalar_tensor_tensor(xT[:, m, :], ps[:, 4 + m % 4, 0:T], mod[:, 40 + m:41 + m], xT[:, m, :], ALU.mult, ALU.add).then_inc(out_done, 1)


def constants():
    import numpy as np
    c = np.zeros((P, N_CONST), np.float32)

    def put(name, a):
        at, w = CONST[name]
        c[0:a.shape[0], at:at + w] = a

    put("ident", np.eye(P, dtype=np.float32))
    r = np.arange(P)
    put("before", (r[:, None] < r[None, :]).astype(np.float32))
    swap = np.zeros((ROPE, ROPE), np.float32)
    h = ROPE // 2
    for m in range(h):
        swap[m + h, m] = -1.0
        swap[m, m + h] = 1.0
    put("swap", np.concatenate([swap, swap], axis=1))
    put("slot_no", np.broadcast_to(np.arange(SLOTS, dtype=np.float32), (P, SLOTS)))
    mask = np.zeros((P, T), np.float32)
    mask[0:CHUNK, T - CHUNK:] = LOW
    put("mask", mask)
    put("group_no", np.broadcast_to(np.arange(GROUPS, dtype=np.float32) - 100, (P, GROUPS)))
    put("expert_no", np.broadcast_to(np.arange(PER_GROUP, dtype=np.float32) - 100, (P, PER_GROUP)))
    inv = np.float32(10000.0) ** (-np.arange(0, ROPE, 2, dtype=np.float32) / np.float32(ROPE))
    put("inv_freq", np.concatenate([inv, inv]).astype(np.float32)[:, None])
    return c


def kernel(**inputs):
    import numpy as np
    import concourse.bacc as bacc
    from concourse.bass_utils import run_bass_kernel_spmd as run

    a = {k: np.asarray(v) for k, v in inputs.items()}

    def cols(x):
        return x.reshape(-1, P).T

    def tiles(w, m):
        return w.reshape(w.shape[0] // P, P, m, P).transpose(1, 2, 0, 3).reshape(P, -1)

    def kcols(w):
        return w.reshape(w.shape[0] // P, P, -1).transpose(1, 0, 2).reshape(P, -1)

    small = np.zeros((P, N_SMALL), np.float32)

    def put(name, x):
        at, w = SMALL[name]
        small[0:x.shape[0], at:at + w] = x

    put("b_ada", cols(a["b_ada"][0]))
    put("g1", cols(a["norm1_g"][0]))
    put("g2", cols(a["norm2_g"][0]))
    put("c", cols(a["c"][0]))
    put("g_qa", cols(a["q_a_norm_g"][0]))
    put("g_kva", cols(a["kv_a_norm_g"][0]))
    put("gq_nope", a["q_norm_g"][0, :NOPE, None])
    put("gk_nope", a["k_norm_g"][0, :NOPE, None])
    put("gq_rope", a["q_norm_g"][0, NOPE:, None])
    put("gk_rope", a["k_norm_g"][0, NOPE:, None])
    put("conv", a["conv_w"][0].reshape(3 * KT, P).T)
    put("b_router", np.broadcast_to(np.concatenate([a["b_router_group"][0], a["b_router_expert"][0]]), (P, 36)))
    put("w_router", kcols(np.concatenate([a["w_router_group"][0], a["w_router_expert"][0]], axis=1)))

    w_in = a["w_in"][0]
    lat0 = 3 * D
    rope0 = lat0 + QL + KVL
    gc0 = rope0 + ROPE
    lat = np.concatenate([tiles(w_in[:, lat0:rope0], LAT_TILES), kcols(w_in[:, rope0:gc0])], axis=1)
    mix = []
    for j in range(HEADS):
        parts = [tiles(w_in[:, o + j * P:o + (j + 1) * P], 1) for o in (0, 2 * D, D, gc0, gc0 + D)]
        parts.append(kcols(a["w_q_b"][0][:, j * QK:(j + 1) * QK]))
        parts.append(kcols(a["w_kv_b"][0][:, j * 256:(j + 1) * 256]))
        mix.append(np.concatenate(parts, axis=1))
    wa = a["w_ada"][0]
    ada = np.stack([tiles(wa[:, n * 512:(n + 1) * 512], ADA_TILES) for n in range(ADA_ITEMS)])
    wo = np.stack([tiles(a["w_o"][0][:, n * 512:(n + 1) * 512], 4) for n in range(2)])
    gate = a["w_exp_gate"][0].reshape(EXPERTS, KT, P, FF).transpose(0, 2, 1, 3).reshape(EXPERTS, P, -1)
    up = a["w_exp_up"][0].reshape(EXPERTS, KT, P, FF).transpose(0, 2, 1, 3).reshape(EXPERTS, P, -1)
    down = a["w_exp_down"][0].reshape(EXPERTS, FF // P, P, D).transpose(0, 2, 1, 3).reshape(EXPERTS, P, -1)
    arrays = {
        "xT": a["x"][0].T.reshape(KT, P, T).transpose(1, 0, 2),
        "pos": np.broadcast_to(a["positions"], (ROPE, T)),
        "small": small,
        "const": constants(),
        "ada": ada,
        "lat": lat,
        "mix": np.stack(mix),
        "wo": wo,
        "gu": np.concatenate([gate, up], axis=2),
        "down": down,
    }
    arrays = {"in_" + k: np.ascontiguousarray(v) for k, v in arrays.items()}
    nc = bacc.Bacc("TRN2", target_bir_lowering=False, num_devices=1)
    aps = [nc.dram_tensor(k, v.shape, mybir.dt.from_np(v.dtype), kind="ExternalInput").ap() for k, v in arrays.items()]
    out = nc.dram_tensor("out_yT", (KT, P, T), F32, kind="ExternalOutput").ap()
    block_kernel(nc, *aps, out)
    r = run(nc, [arrays], core_ids=[0])
    y = np.asarray(r.results[0]["out_yT"])
    return np.ascontiguousarray(y.reshape(D, T).T).reshape(1, T, D)
```

```python
from contextlib import ExitStack

import concourse.bass as bass
from concourse import mybir

F32 = mybir.dt.float32
I32 = mybir.dt.int32
ACT = mybir.ActivationFunctionType
ALU = mybir.AluOpType
AX_X = mybir.AxisListType.X
PI = 3.14159265358979

P = 128
D = 1024
T = 256
KT = D // P
TT = T // P
HEADS = 8
NOPE, ROPE = 128, 64
QK = NOPE + ROPE
QL, KVL = 384, 256
GROUPS, PER_GROUP = 4, 8
EXPERTS = GROUPS * PER_GROUP
FF = 256
SLOTS = 2 * T
WIN = 32
EPS = 1e-6
LOW = -1.0e30
CHUNK = 64

SMALL_WIDTHS = (("b_ada", 48), ("g1", KT), ("g2", KT), ("c", KT), ("g_qa", 3), ("g_kva", 2),
                ("gq_nope", 1), ("gk_nope", 1), ("gq_rope", 1), ("gk_rope", 1), ("conv", 3 * KT),
                ("b_router", 36), ("w_router", KT * 36))
CONST_WIDTHS = (("ident", P), ("before", P), ("swap", P), ("slot_no", SLOTS), ("mask", T),
                ("group_no", GROUPS), ("expert_no", PER_GROUP), ("inv_freq", 1))


def places(widths):
    at, out = 0, {}
    for name, width in widths:
        out[name] = (at, width)
        at += width
    return out, at


SMALL, N_SMALL = places(SMALL_WIDTHS)
CONST, N_CONST = places(CONST_WIDTHS)

ADA_ITEMS, ADA_TILES = 12, 4
ADA_COLS = KT * ADA_TILES * P
LAT_TILES = 5
LAT_COLS = KT * (LAT_TILES * P + ROPE)
CONV_COLS = KT * 5 * P
WQ_AT = CONV_COLS
WKV_AT = WQ_AT + 3 * QK
MIX_COLS = WKV_AT + 2 * 256
WO_COLS = KT * 4 * P
GU_COLS = 2 * KT * FF
DOWN_COLS = (FF // P) * D
EX_SLOTS = 4
WINDOWS = EXPERTS + SLOTS // WIN
YW = SLOTS + WIN


def block_kernel(nc, xT_d, pos_d, small_d, const_d, ada_d, lat_d, mix_d, wo_d, gu_d, down_d, out_d):
    with ExitStack() as ctx:
        def sb(name, shape, dt=F32):
            return ctx.enter_context(nc.sbuf_tensor(name, shape, dt))

        def sem(name):
            return ctx.enter_context(nc.semaphore(name))

        ps = ctx.enter_context(nc.psum_tensor("ps", [P, 8, 512], F32))

        wex = sb("wex", [P, EX_SLOTS, GU_COLS + DOWN_COLS])
        wmix = sb("wmix", [P, 2, MIX_COLS])
        wmix_flat = wmix[:].rearrange("p a b -> p (a b)")
        xg = wmix_flat[:, 0:KT * YW].rearrange("p (k s) -> p k s", k=KT)
        yT = wmix_flat[:, KT * YW:2 * KT * YW].rearrange("p (k s) -> p k s", k=KT)
        xT = sb("xT", [P, KT, T])
        act2 = sb("act2", [P, 2 * KT, T])
        hT = act2[:, 0:KT, :]
        merged = act2[:, KT:2 * KT, :]
        h2_rows = merged.rearrange("p (t a) n -> p t (a n)", t=TT)
        y_rows = act2[:].rearrange("p k n -> p (k n)")
        small = sb("small", [P, N_SMALL])
        const = sb("const", [P, N_CONST])
        ones = sb("ones", [P, P])
        eps_q = sb("eps_q", [P, 1])
        eps_1 = sb("eps_1", [P, 1])
        c_rep = sb("c_rep", [P, KT, WIN])
        mod = sb("mod", [P, 48])
        a12 = sb("a12", [P, 2, KT])
        cos_t = sb("cos_t", [ROPE, T])
        sin_t = sb("sin_t", [ROPE, T])
        k_rot = sb("k_rot", [ROPE, T])
        k_rope_sq = sb("k_rope_sq", [ROPE, T])
        work = sb("work", [P, 6850])
        work_at = [0]

        def piece(cols, parts=P):
            a = work_at[0]
            work_at[0] += cols
            assert work_at[0] <= 6850
            return work[0:parts, a:a + cols]

        q_lat = piece(3 * T).rearrange("p (k n) -> p k n", k=3)
        kv_lat = piece(2 * T).rearrange("p (k n) -> p k n", k=2)
        q_sq = piece(T)
        k_sq = piece(T)
        q_n = piece(T)
        q_x = piece(T, ROPE)
        q_r = piece(T, ROPE)
        rope_t = piece(T, ROPE)
        qr_sq = rope_t
        k_n = piece(T)
        k_r = piece(T, ROPE)
        v_sb = piece(2 * P).rearrange("p (a b) -> p a b", a=2)
        rms = piece(2 * T)
        rk_s, rk = rms[:, 0:T], rms[:, T:2 * T]
        scores = piece(P + T)
        probs = piece(P + T)
        pT = piece(P + T)
        zx = piece(T)
        t_gate = piece(T)
        m_gate = piece(T)
        conv_t = piece(T)
        y_conv = piece(T)
        o_t = zx
        u = piece(T + 2)
        stat = piece(16)
        wk_rows = work[:, 0:2 * 512]
        posi, posf = q_x.bitcast(I32), k_r
        work_at[0] = 0
        sel = piece(TT * SLOTS).rearrange("p (t s) -> p t s", t=TT)
        sel_w = piece(TT * SLOTS).rearrange("p (t s) -> p t s", t=TT)
        comb_t = piece(SLOTS)
        xw = piece(KT * WIN).rearrange("p (k n) -> p k n", k=KT)
        gu_sb = piece(P)
        silu_t = piece(2 * WIN)
        act_t = piece(2 * WIN)
        d_sb = piece(T)
        wins = piece(3 * EXPERTS)
        comb = piece(4 * T).rearrange("p (s n) -> p s n", s=4)
        lg = piece(72).rearrange("p (t n) -> p t n", t=TT)
        r2s = piece(T)
        r2 = piece(T)
        g_work = piece(5 * 8).rearrange("p (a t n) -> p a t n", a=5, t=TT)
        e_work = piece(6 * 16).rearrange("p (a t n) -> p a t n", a=6, t=TT)
        s_work = piece(24).rearrange("p (a t) -> p a t", a=12)
        oh = piece(4 * 64).rearrange("p (a t n) -> p a t n", a=4, t=TT)
        pos_e = piece(64).rearrange("p (t n) -> p t n", t=TT)
        cnt = piece(EXPERTS)
        incl = piece(EXPERTS)
        offf = piece(EXPERTS)
        table = sb("table", [1, 3 * EXPERTS], I32)
        ada_rows = [wk_rows[:, 0:512], wk_rows[:, 512:1024]]

        def sm(name, i=0, n=None, parts=P):
            a, w = SMALL[name]
            return small[0:parts, a + i:a + i + (n or w)]

        def co(name, parts=P):
            a, w = CONST[name]
            return const[0:parts, a:a + w]

        ident, before = co("ident"), co("before")

        x_landed, small_landed, const_landed, pos_landed = sem("x_landed"), sem("small_landed"), sem("const_landed"), sem("pos_landed")
        mix_landed = [sem("mix_landed0"), sem("mix_landed1")]
        ada_done = sem("ada_done")
        gu_landed = [sem(f"gu_landed{s}") for s in range(EX_SLOTS)]
        down_landed = [sem(f"down_landed{s}") for s in range(EX_SLOTS)]
        dve_step = sem("dve_step")
        act_step = sem("act_step")
        setup_done = sem("setup_done")
        c_ready, xsq_ready, xss_ready, r1_ready = sem("c_ready"), sem("xsq_ready"), sem("xss_ready"), sem("r1_ready")
        h_ready = sem("h_ready")
        lat_ready, lat_sq_ready, lat_ss_ready, lat_rms_ready = sem("lat_ready"), sem("lat_sq_ready"), sem("lat_ss_ready"), sem("lat_rms_ready")
        angles_ready, trig_ready = sem("angles_ready"), sem("trig_ready")
        krope_ready, kswap_ready, lat_norm_ready = sem("krope_ready"), sem("kswap_ready"), sem("lat_norm_ready")
        qk_ready, qr_ready, v_ready = sem("qk_ready"), sem("qr_ready"), sem("v_ready")
        sq_ready, v_copied, qx_ready = sem("sq_ready"), sem("v_copied"), sem("qx_ready")
        kss_ready, qss_ready, swap_ready = sem("kss_ready"), sem("qss_ready"), sem("swap_ready")
        rk_sqrt, qs_sqrt, kq_ready = sem("rk_sqrt"), sem("qs_sqrt"), sem("kq_ready")
        zxc_ready, zx_copied, u_done = sem("zxc_ready"), sem("zx_copied"), sem("u_done")
        s_ready, max_ready, exp_done, p_ready = sem("s_ready"), sem("max_ready"), sem("exp_done"), sem("p_ready")
        zbg_ready, conv_gate_ready, y_done = sem("zbg_ready"), sem("conv_gate_ready"), sem("y_done")
        pT_ready, pT_copied = sem("pT_ready"), sem("pT_copied")
        zgm_ready, mla_gate_ready = sem("zgm_ready"), sem("mla_gate_ready")
        o_ready, merged_ready = sem("o_ready"), sem("merged_ready")
        wo_ready, x2_ready, x2sq_ready, x2ss_ready, r2_ready, h2_ready = (sem("wo_ready"), sem("x2_ready"), sem("x2sq_ready"), sem("x2ss_ready"), sem("r2_ready"), sem("h2_ready"))
        lg_ready, h2r_ready, h2r_copied = sem("lg_ready"), sem("h2r_ready"), sem("h2r_copied")
        gdiff_ready, gexp_ready, ediff_ready, eexp_ready = sem("gdiff_ready"), sem("gexp_ready"), sem("ediff_ready"), sem("eexp_ready")
        onehot_ready, rank_ready, table_ready, sel_ready, comb_rows_ready = (sem("onehot_ready"), sem("rank_ready"), sem("table_ready"), sem("sel_ready"), sem("comb_rows_ready"))
        pad_done = sem("pad_done")
        xg_ready, xg_act, xg_dve = sem("xg_ready"), sem("xg_act"), sem("xg_dve")
        comb_ready, comb_copied = sem("comb_ready"), sem("comb_copied")
        ada_copied, ada_turned = sem("ada_copied"), sem("ada_turned")
        xw_ready, gu_ready, gu_copied, gu_turned = sem("xw_ready"), sem("gu_ready"), sem("gu_copied"), sem("gu_turned")
        silu_done, act_done, down_ready, down_copied = sem("silu_done"), sem("act_done"), sem("down_ready"), sem("down_copied")
        down_turned, y_done2 = sem("down_turned"), sem("y_stored")
        yr_ready, yr_copied, out_ready, out_done, out_stored = (sem("yr_ready"), sem("yr_copied"), sem("out_ready"), sem("out_done"), sem("out_stored"))

        MIX0 = 5
        ADA2 = MIX0 + HEADS
        WO0 = ADA2 + 8
        block = ctx.enter_context(nc.Block())

        def window_table(eng, e):
            off = eng.value_load(table[0:1, bass.ds(e, 1)], min_val=0, max_val=SLOTS)
            at = eng.value_load(table[0:1, bass.ds(e + EXPERTS, 1)], min_val=0, max_val=WINDOWS)
            upto = eng.value_load(table[0:1, bass.ds(e + 2 * EXPERTS, 1)], min_val=1, max_val=WINDOWS)
            return off, at, upto

        @block.sync
        def _(sp):
            sp.dma_start(xT[:], xT_d).then_inc(x_landed, 16)
            sp.dma_start(small[:], small_d).then_inc(small_landed, 16)
            sp.dma_start(const[:], const_d).then_inc(const_landed, 16)
            sp.dma_start(posi, pos_d).then_inc(pos_landed, 16)

            def ring(n, dst_cols, src):
                before_it = n - 2
                if 0 <= before_it < 4:
                    sp.wait_ge(ada_done, before_it + 1)
                elif before_it == 4:
                    sp.wait_ge(lat_ready, 1)
                elif MIX0 <= before_it < ADA2:
                    sp.wait_ge(zgm_ready, before_it - MIX0 + 1)
                elif before_it >= ADA2:
                    sp.wait_ge(ada_done, before_it - ADA2 + 5)
                sp.dma_start(wmix[:, n % 2, 0:dst_cols], src).then_inc(mix_landed[n % 2], 16)

            for n in range(4):
                ring(n, ADA_COLS, ada_d[n])
            ring(4, LAT_COLS, lat_d)
            for j in range(HEADS):
                ring(MIX0 + j, MIX_COLS, mix_d[j])
                if 1 <= j <= EX_SLOTS:
                    s = j - 1
                    sp.dma_start(wex[:, s, 0:GU_COLS], gu_d[s]).then_inc(gu_landed[s], 16)
                    sp.dma_start(wex[:, s, GU_COLS:], down_d[s]).then_inc(down_landed[s], 16)
            for n in range(8):
                ring(ADA2 + n, ADA_COLS, ada_d[4 + n])
            for n in range(2):
                ring(WO0 + n, WO_COLS, wo_d[n])
            sp.wait_ge(table_ready, 1)
            with sp.Fori(0, EXPERTS // EX_SLOTS - 1) as i:
                for s in range(EX_SLOTS):
                    upto = sp.value_load(table[0:1, bass.ds(i * EX_SLOTS + (s + 2 * EXPERTS), 1)], min_val=1, max_val=WINDOWS)
                    sp.wait_ge(gu_ready, upto + 1)
                    sp.dma_start(wex[:, s, 0:GU_COLS], gu_d[bass.ds(i * EX_SLOTS + (s + EX_SLOTS), 1)].rearrange("a p c -> p (a c)")).then_inc(gu_landed[s], 16)
                    sp.wait_ge(down_ready, upto)
                    sp.dma_start(wex[:, s, GU_COLS:], down_d[bass.ds(i * EX_SLOTS + (s + EX_SLOTS), 1)].rearrange("a p c -> p (a c)")).then_inc(down_landed[s], 16)
            for m in range(KT):
                sp.wait_ge(out_done, m + 1)
                sp.dma_start(out_d[m], xT[:, m, :]).then_inc(out_stored, 16)
            sp.wait_ge(out_stored, 16 * KT)

        @block.gpsimd
        def _(pool):
            pool.wait_ge(wo_ready, 2)
            nc.gpsimd.memset(xg[:, :, SLOTS:YW], 0.0).then_inc(pad_done, 1)
            pool.wait_ge(pad_done, 1)
            pool.wait_ge(table_ready, 1)
            pool.wait_ge(xg_act, 4)
            pool.wait_ge(xg_dve, 4)
            with pool.Fori(0, EXPERTS) as e:
                off, at, upto = window_table(pool, e)
                with pool.Fori(0, upto - at) as w:
                    pool.wait_ge(gu_ready, at + w + 1)
                    win_at = nc.s_assert_within(off + w * WIN, 0, SLOTS, skip_runtime_bounds_check_because="a window starts before the last slot of its expert")
                    nc.gpsimd.tensor_copy(xw, xg[:, :, bass.ds(win_at, WIN)]).then_inc(xw_ready, 1)

        @block.scalar
        def _(act):
            act.wait_ge(small_landed, 16)
            nc.scalar.activation(c_rep[:], sm("c").unsqueeze(2).broadcast_to([P, KT, WIN]), ACT.Silu).then_inc(c_ready, 1)
            act.wait_ge(x_landed, 16)
            nc.scalar.activation(merged, xT[:], ACT.Square).then_inc(xsq_ready, 1)
            act.wait_ge(angles_ready, 1)
            nc.scalar.activation(sin_t[:], sin_t[:], ACT.Sin)
            nc.scalar.activation(cos_t[:], cos_t[:], ACT.Sin).then_inc(trig_ready, 1)
            act.wait_ge(xss_ready, 1)
            act.wait_ge(setup_done, 4)
            nc.scalar.activation(rms[:, 0:T], ps[:, 3, 0:T], ACT.Sqrt, bias=eps_1[:], scale=1.0 / D).then_inc(r1_ready, 1)

            act.wait_ge(ada_done, 4)
            nc.scalar.copy(act2[:, 8:10, :].rearrange("p a n -> p (a n)"), ps[:, 0, :]).then_inc(ada_copied, 1)

            act.wait_ge(lat_ready, 1)
            nc.scalar.activation(merged[:, 0:2, :], ps[:, 1, :], ACT.Square)
            nc.scalar.activation(merged[:, 2:4, :], ps[:, 2, :], ACT.Square)
            nc.scalar.activation(merged[:, 4, :], ps[:, 4, 0:T], ACT.Square)
            nc.scalar.activation(k_rope_sq[:], ps[0:ROPE, 4, T:2 * T], ACT.Square).then_inc(lat_sq_ready, 1)
            act.wait_ge(lat_ss_ready, 1)
            nc.scalar.activation(rms[:, 0:T], ps[:, 3, 0:T], ACT.Sqrt, bias=eps_1[:], scale=1.0 / QL)
            nc.scalar.activation(rms[:, T:2 * T], ps[:, 3, T:2 * T], ACT.Sqrt, bias=eps_1[:], scale=1.0 / KVL).then_inc(lat_rms_ready, 1)

            with act.Fori(0, HEADS // 2) as i:
                for half in range(2):
                    n = i * 2 + (half + 1)
                    act.wait_ge(qk_ready, n)
                    nc.scalar.activation(q_sq, ps[:, 0, 0:T], ACT.Square)
                    nc.scalar.activation(k_sq, ps[:, 0, T:2 * T], ACT.Square)
                    act.wait_ge(qr_ready, n)
                    nc.scalar.activation(qr_sq, ps[0:ROPE, 1, 0:T], ACT.Square).then_inc(sq_ready, 1)
                    act.wait_ge(v_ready, n)
                    nc.scalar.copy(v_sb, ps[:, 2, 0:2 * P].rearrange("p (a b) -> p a b", a=2)).then_inc(v_copied, 1)
                    act.wait_ge(kss_ready, n)
                    nc.scalar.activation(rk_s, ps[:, 3, 0:T], ACT.Sqrt, bias=eps_1[:], scale=1.0 / QK).then_inc(rk_sqrt, 1)
                    act.wait_ge(qss_ready, n)
                    nc.scalar.activation(stat[:, 0:2], ps[:, 4, 0:2], ACT.Sqrt, bias=eps_q[:], scale=1.0).then_inc(qs_sqrt, 1)
                    act.wait_ge(zxc_ready, n)
                    nc.scalar.copy(zx, ps[:, 5, 0:T]).then_inc(zx_copied, 1)
                    act.wait_ge(max_ready, n + 1)
                    nc.scalar.activation(probs[:, 0:P], scores[:, 0:P], ACT.Exp, bias=stat[:, 6:7], scale=stat[:, 2:3], accum_out=stat[:, 8:9])
                    nc.scalar.activation(probs[:, P:P + T], scores[:, P:P + T], ACT.Exp, bias=stat[:, 7:8], scale=stat[:, 3:4], accum_out=stat[:, 9:10]).then_inc(exp_done, 1)
                    act.wait_ge(zbg_ready, n)
                    nc.scalar.activation(t_gate, ps[:, 6, T:2 * T], ACT.Tanh, scale=0.5).then_inc(conv_gate_ready, 1)
                    act.wait_ge(pT_ready, n)
                    nc.scalar.copy(pT, ps[:, 4, 0:P + T]).then_inc(pT_copied, 1)
                    act.wait_ge(zgm_ready, n)
                    nc.scalar.activation(m_gate, ps[:, 7, 0:T], ACT.Tanh, scale=0.5).then_inc(mla_gate_ready, 1)

            for b in range(2):
                act.wait_ge(ada_done, 8 + 4 * b)
                nc.scalar.copy(ada_rows[b], ps[:, 5 + b, :]).then_inc(ada_copied, 1)
            for a in range(2):
                act.wait_ge(x2_ready, a + 1)
                act.wait_ge(wo_ready, 2)
                nc.scalar.activation(hT[:, 4 * a:4 * a + 4, :], xT[:, 4 * a:4 * a + 4, :], ACT.Square).then_inc(x2sq_ready, 1)
            act.wait_ge(x2ss_ready, 1)
            nc.scalar.activation(r2s, ps[:, 5, 0:T], ACT.Sqrt, bias=eps_1[:], scale=1.0 / D).then_inc(r2_ready, 1)
            for b in range(4):
                act.wait_ge(h2r_ready, b + 1)
                nc.scalar.copy(h2_rows[:, b // 2, (b % 2) * 512:(b % 2) * 512 + 512], ps[:, 1 + b, :]).then_inc(h2r_copied, 1)
                if b == 1:
                    act.wait_ge(gdiff_ready, 1)
                    nc.scalar.activation(g_work[:, 1], g_work[:, 1], ACT.Exp).then_inc(gexp_ready, 1)
            act.wait_ge(ediff_ready, 1)
            nc.scalar.activation(s_work[:, 6, :], s_work[:, 5, :], ACT.Exp).then_inc(eexp_ready, 1)
            for k in range(0, KT, 2):
                act.wait_ge(xg_ready, k + 1)
                nc.scalar.copy(xg[:, k, 0:SLOTS], ps[:, k, :]).then_inc(xg_act, 1)
            act.wait_ge(comb_ready, 1)
            nc.scalar.copy(comb, ps[:, 2:4, :].rearrange("p b (s n) -> p (b s) n", s=2)).then_inc(comb_copied, 1)

            act.wait_ge(table_ready, 1)
            act.sem_inc(y_done2, 1)
            with act.Fori(0, EXPERTS) as e:
                off, at, upto = window_table(act, e)
                with act.Fori(0, upto - at) as w:
                    n = at + w + 1
                    act.wait_ge(gu_ready, n + 1)
                    nc.scalar.copy(gu_sb, ps[:, 0, 0:P]).then_inc(gu_copied, 1)
                    act.wait_ge(gu_turned, n)
                    nc.scalar.activation(silu_t, ps[:, 1, 0:2 * WIN], ACT.Silu).then_inc(silu_done, 1)
                    win_at = nc.s_assert_within(off + w * WIN, 0, SLOTS, skip_runtime_bounds_check_because="a window starts before the last slot of its expert")
                    act.wait_ge(down_turned, n)
                    nc.scalar.copy(yT.rearrange("p (c h) s -> p c h s", c=4)[:, :, :, bass.ds(win_at, WIN)],
                                   ps[:, 3, 0:2 * P].rearrange("p (h c n) -> p c h n", h=2, c=4)).then_inc(y_done2, 1)
            for m in range(KT):
                act.wait_ge(yr_ready, m + 1)
                nc.scalar.copy(y_rows[:, (m % 2) * 512:(m % 2) * 512 + 512], ps[:, m % 2, :]).then_inc(yr_copied, 1)

        @block.tensor
        def _(pe):
            def mm(out, lhsT, rhs, start, stop, **kw):
                return nc.tensor.matmul(out, lhsT, rhs, start=start, stop=stop, **kw)

            pe.wait_ge(setup_done, 4)
            pe.wait_ge(xsq_ready, 1)
            for k in range(KT):
                last = mm(ps[:, 3, 0:T], ones[:], merged[:, k, :], k == 0, k == KT - 1)
            last.then_inc(xss_ready, 1)

            def ada_item(slot, out):
                w = wmix[:, slot, 0:ADA_COLS].rearrange("p (k c) -> p k c", k=KT)
                for k in range(KT):
                    for q in range(4):
                        last = mm(out[q * WIN:(q + 1) * WIN, :], c_rep[:, k, :], w[:, k, q * P:(q + 1) * P], k == 0, k == KT - 1)
                return last

            def ada_turn(rows, out):
                for a in range(4):
                    last = nc.tensor.transpose(out[:, a * P:(a + 1) * P], rows[:, a * P:(a + 1) * P], ident)
                return last

            pe.wait_ge(c_ready, 1)
            for n in range(4):
                pe.wait_ge(mix_landed[n % 2], 16 * (n // 2 + 1))
                ada_item(n % 2, ps[:, 0, n * P:(n + 1) * P]).then_inc(ada_done, 1)
            pe.wait_ge(ada_copied, 1)
            ada_turn(act2[:, 8:10, :].rearrange("p a n -> p (a n)"), ps[:, 1, :]).then_inc(ada_turned, 1)

            pe.wait_ge(mix_landed[0], 16 * 3)
            pe.wait_ge(h_ready, KT)
            w = wmix[:, 0, 0:KT * LAT_TILES * P].rearrange("p (m k c) -> p m k c", m=LAT_TILES, k=KT)
            wr = wmix[:, 0, KT * LAT_TILES * P:LAT_COLS].rearrange("p (k c) -> p k c", k=KT)
            lat_ps = [ps[:, 1, 0:T], ps[:, 1, T:2 * T], ps[:, 2, 0:T], ps[:, 2, T:2 * T], ps[:, 4, 0:T]]
            for m in range(LAT_TILES):
                for k in range(KT):
                    mm(lat_ps[m], w[:, m, k, :], hT[:, k, :], k == 0, k == KT - 1)
            for k in range(KT):
                last = mm(ps[0:ROPE, 4, T:2 * T], wr[:, k, :], hT[:, k, :], k == 0, k == KT - 1)
            last.then_inc(lat_ready, 1)
            pe.wait_ge(lat_sq_ready, 1)
            for k in range(3):
                mm(ps[:, 3, 0:T], ones[:], merged[:, k, :], k == 0, k == 2)
            for k in range(2):
                last = mm(ps[:, 3, T:2 * T], ones[:], merged[:, 3 + k, :], k == 0, k == 1)
            last.then_inc(lat_ss_ready, 1)
            pe.wait_ge(krope_ready, 1)
            mm(ps[:, 5, 0:T], co("swap", ROPE), k_r, True, True).then_inc(kswap_ready, 1)
            pe.wait_ge(lat_norm_ready, 1)

            with pe.Fori(0, HEADS // 2) as i:
                for half in range(2):
                    done = i * 2 + half
                    slot = (MIX0 + half) % 2
                    w = wmix[:, slot, 0:CONV_COLS].rearrange("p (m k c) -> p m k c", m=5, k=KT)
                    wq = wmix[:, slot, WQ_AT:WKV_AT].rearrange("p (k c) -> p k c", k=3)
                    wkv = wmix[:, slot, WKV_AT:MIX_COLS].rearrange("p (k c) -> p k c", k=2)

                    def conv_tile(m, out):
                        for k in range(KT):
                            last = mm(out, w[:, m, k, :], hT[:, k, :], k == 0, k == KT - 1)
                        return last

                    pe.wait_ge(mix_landed[slot], i * 16 + 16 * ((MIX0 + half) // 2 + 1))
                    pe.wait_ge(kq_ready, done + 1)
                    for k in range(3):
                        mm(ps[:, 0, 0:T], wq[:, k, 0:NOPE], q_lat[:, k, :], k == 0, k == 2)
                    for k in range(2):
                        last = mm(ps[:, 0, T:2 * T], wkv[:, k, 0:NOPE], kv_lat[:, k, :], k == 0, k == 1)
                    last.then_inc(qk_ready, 1)
                    for k in range(3):
                        last = mm(ps[0:ROPE, 1, 0:T], wq[:, k, NOPE:QK], q_lat[:, k, :], k == 0, k == 2)
                    last.then_inc(qr_ready, 1)
                    pe.wait_ge(merged_ready, done + 1)
                    for t in range(TT):
                        for k in range(2):
                            last = mm(ps[:, 2, t * P:(t + 1) * P], kv_lat[:, k, t * P:(t + 1) * P], wkv[:, k, NOPE:], k == 0, k == 1)
                    last.then_inc(v_ready, 1)
                    pe.wait_ge(u_done, done + 1)
                    conv_tile(0, ps[:, 5, 0:T])
                    pe.wait_ge(sq_ready, done + 1)
                    pe.wait_ge(max_ready, done + 1)
                    mm(ps[:, 3, 0:T], ones[:], k_sq, True, False)
                    mm(ps[:, 3, 0:T], ones[0:ROPE, :], k_rope_sq[:], False, True).then_inc(kss_ready, 1)
                    for t in range(TT):
                        mm(ps[:, 4, t:t + 1], q_sq[:, t * P:(t + 1) * P], ones[:, 0:1], True, False)
                        last = mm(ps[:, 4, t:t + 1], qr_sq[:, t * P:(t + 1) * P], ones[0:ROPE, 0:1], False, True)
                    last.then_inc(qss_ready, 1)
                    pe.wait_ge(qx_ready, done + 1)
                    mm(ps[:, 1, T:2 * T], co("swap", ROPE), q_x, True, True).then_inc(swap_ready, 1)
                    conv_tile(1, ps[:, 5, T:2 * T]).then_inc(zxc_ready, 1)
                    pe.wait_ge(kq_ready, done + 2)
                    pe.wait_ge(rk_sqrt, done + 1)
                    mm(ps[:, 3, 0:P], q_n[:, 0:P], k_n[:, 0:P], True, False)
                    mm(ps[:, 3, 0:P], q_r[:, 0:P], k_r[:, 0:P], False, True)
                    mm(ps[:, 3, P:P + T], q_n[:, P:T], k_n, True, False)
                    mm(ps[:, 3, P:P + T], q_r[:, P:T], k_r, False, True).then_inc(s_ready, 1)
                    pe.wait_ge(y_done, done + 1)
                    conv_tile(2, ps[:, 6, 0:T])
                    conv_tile(3, ps[:, 6, T:2 * T]).then_inc(zbg_ready, 1)
                    pe.wait_ge(p_ready, done + 1)
                    nc.tensor.transpose(ps[:, 4, 0:P], probs[:, 0:P], ident)
                    nc.tensor.transpose(ps[:, 4, P:2 * P], probs[:, P:2 * P], ident)
                    nc.tensor.transpose(ps[:, 4, 2 * P:3 * P], probs[:, 2 * P:3 * P], ident).then_inc(pT_ready, 1)
                    conv_tile(4, ps[:, 7, 0:T]).then_inc(zgm_ready, 1)
                    pe.wait_ge(pT_copied, done + 1)
                    mm(ps[:, 2, T:2 * T], v_sb[:, 0, :], pT[:, 0:T], True, False)
                    mm(ps[:, 2, T + P:2 * T], v_sb[:, 1, :], pT[:, T:T + P], False, True).then_inc(o_ready, 1)

            pe.wait_ge(y_done, HEADS + 1)
            pe.wait_ge(u_done, HEADS + 1)
            for n in range(4, ADA_ITEMS):
                item = ADA2 + n - 4
                pe.wait_ge(mix_landed[item % 2], 16 * (item // 2 + 1))
                ada_item(item % 2, ps[:, 4 + n // 4, (n % 4) * P:(n % 4 + 1) * P]).then_inc(ada_done, 1)
            for b in range(2):
                pe.wait_ge(ada_copied, b + 2)
                if b == 0:
                    pe.wait_ge(merged_ready, HEADS + 1)
                ada_turn(ada_rows[b], ps[:, 7 if b == 0 else 0, :]).then_inc(ada_turned, 1)

            pe.wait_ge(merged_ready, HEADS + 1)
            for a in range(2):
                slot = (WO0 + a) % 2
                pe.wait_ge(mix_landed[slot], 16 * ((WO0 + a) // 2 + 1))
                w = wmix[:, slot, 0:WO_COLS].rearrange("p (m k c) -> p m k c", m=4, k=KT)
                for m in range(4):
                    for k in range(KT):
                        last = mm(ps[:, 1 + 2 * a + m // 2, (m % 2) * T:(m % 2 + 1) * T], w[:, m, k, :], merged[:, k, :], k == 0, k == KT - 1)
                last.then_inc(wo_ready, 1)
            for k in range(KT):
                if k % 4 == 0:
                    pe.wait_ge(x2sq_ready, k // 4 + 1)
                last = mm(ps[:, 5, 0:T], ones[:], hT[:, k, :], k == 0, k == KT - 1)
            last.then_inc(x2ss_ready, 1)

            pe.wait_ge(h2_ready, KT)
            a0 = SMALL["w_router"][0]
            for t in range(TT):
                for k in range(KT):
                    last = mm(ps[:, 6, 64 * t:64 * t + 36], hT[:, k, t * P:(t + 1) * P], small[:, a0 + 36 * k:a0 + 36 * k + 36], k == 0, k == KT - 1)
            last.then_inc(lg_ready, 1)
            for b in range(4):
                for q in range(4):
                    last = nc.tensor.transpose(ps[:, 1 + b, q * P:(q + 1) * P], hT[:, (b % 2) * 4 + q, (b // 2) * P:(b // 2 + 1) * P], ident)
                last.then_inc(h2r_ready, 1)
            pe.wait_ge(onehot_ready, 1)
            mm(ps[:, 7, 0:32], before, oh[:, 2, 0, :], True, True)
            mm(ps[:, 7, 32:64], ones[:], oh[:, 2, 0, :], True, False)
            mm(ps[:, 7, 32:64], before, oh[:, 2, 1, :], False, True)
            mm(ps[:, 7, 64:96], ones[:], oh[:, 2, 0, :], True, False)
            mm(ps[:, 7, 64:96], ones[:], oh[:, 2, 1, :], False, True).then_inc(rank_ready, 1)
            pe.wait_ge(h2r_copied, 4)
            pe.wait_ge(sel_ready, 2)
            for k in range(KT):
                for t in range(TT):
                    last = mm(ps[:, k, :], h2_rows[:, t, k * P:(k + 1) * P], sel[:, t, :], t == 0, t == TT - 1)
                last.then_inc(xg_ready, 1)
            pe.wait_ge(comb_rows_ready, 2)
            pe.wait_ge(xg_act, 2)
            pe.wait_ge(xg_dve, 2)
            for s in range(4):
                for t in range(TT):
                    c0 = (s % 2) * T + t * P
                    last = nc.tensor.transpose(ps[:, 2 + s // 2, c0:c0 + P], sel_w[:, t, s * P:(s + 1) * P], ident)
            last.then_inc(comb_ready, 1)

            pe.wait_ge(xg_act, 4)
            pe.wait_ge(xg_dve, 4)
            pe.wait_ge(comb_copied, 1)
            pe.wait_ge(table_ready, 1)
            pe.sem_inc(gu_ready, 1)
            with pe.Fori(0, EXPERTS // EX_SLOTS) as i:
                for s in range(EX_SLOTS):
                    off, at, upto = window_table(pe, i * EX_SLOTS + s)
                    wgu = wex[:, s, 0:GU_COLS].rearrange("p (k c) -> p k c", k=KT)
                    wdn = wex[:, s, GU_COLS:].rearrange("p (f c) -> p f c", f=2)
                    with pe.Fori(0, upto - at) as w:
                        n = at + w + 1
                        pe.wait_ge(gu_landed[s], i * 16 + 16)
                        pe.wait_ge(xw_ready, n)
                        for k in range(KT):
                            for q in range(4):
                                last = mm(ps[q * WIN:(q + 1) * WIN, 0, 0:P], xw[:, k, :], wgu[:, k, q * P:(q + 1) * P], k == 0, k == KT - 1)
                        last.then_inc(gu_ready, 1)
                        pe.wait_ge(gu_copied, n)
                        nc.tensor.transpose(ps[:, 1, 0:P], gu_sb, ident).then_inc(gu_turned, 1)
                        pe.wait_ge(down_landed[s], i * 16 + 16)
                        pe.wait_ge(act_done, n)
                        for f in range(2):
                            for q in range(4):
                                last = mm(ps[q * WIN:(q + 1) * WIN, 2, 0:T], act_t[:, f * WIN:(f + 1) * WIN], wdn[:, f, q * T:(q + 1) * T], f == 0, f == 1)
                        last.then_inc(down_ready, 1)
                        pe.wait_ge(y_done2, n)
                        pe.wait_ge(down_copied, n)
                        nc.tensor.transpose(ps[:, 3, 0:P], d_sb[:, 0:P], ident)
                        nc.tensor.transpose(ps[:, 3, P:2 * P], d_sb[:, P:2 * P], ident).then_inc(down_turned, 1)

            last_window = pe.value_load(table[0:1, 3 * EXPERTS - 1:3 * EXPERTS], min_val=1, max_val=WINDOWS)
            pe.wait_ge(y_done2, last_window + 1)

            def turn(m):
                if m >= 2:
                    pe.wait_ge(yr_copied, m - 1)
                for t in range(4):
                    last = nc.tensor.transpose(ps[:, m % 2, t * P:(t + 1) * P], yT[:, m, t * P:(t + 1) * P], ident)
                last.then_inc(yr_ready, 1)

            turn(0)
            for m in range(KT):
                if m + 1 < KT:
                    turn(m + 1)
                pe.wait_ge(yr_copied, m + 1)
                if m >= 4:
                    pe.wait_ge(out_done, m - 3)
                for t in range(4):
                    c0 = (m % 2) * 512 + t * P
                    last = mm(ps[:, 4 + m % 4, 0:T], y_rows[:, c0:c0 + P], comb[:, t, :], t == 0, t == 3)
                last.then_inc(out_ready, 1)

        @block.vector
        def _(dve):
            v = nc.vector
            chain = [0, None]

            def step_value(k):
                return k if chain[1] is None else chain[1] + k

            def link(ins):
                chain[0] += 1
                ins.then_inc(dve_step, 1)
                dve.wait_ge(dve_step, step_value(chain[0]))

            v.memset(ones[:], 1.0).then_inc(setup_done, 1)
            v.memset(eps_1[:], EPS).then_inc(setup_done, 1)
            v.memset(eps_q[:], EPS * QK).then_inc(setup_done, 1)
            v.memset(u, 0.0).then_inc(setup_done, 1)

            C1 = 6.28125
            C2 = 0.0019350051879882812
            C3 = 2 * 3.141592653589793 - C1 - C2
            MAGIC = 1.5 * 2.0 ** 23
            dve.wait_ge(pos_landed, 16)
            dve.wait_ge(const_landed, 16)
            link(v.tensor_copy(posf, posi))
            link(v.tensor_scalar(posf, posf, co("inv_freq", ROPE), None, ALU.mult))
            for out, quarter in ((sin_t, 0.0), (cos_t, 0.25)):
                link(v.tensor_scalar(out[:], posf, 1.0 / (2 * PI), quarter, ALU.mult, ALU.add))
                link(v.tensor_scalar(out[:], out[:], MAGIC, None, ALU.add))
                link(v.tensor_scalar(out[:], out[:], MAGIC, None, ALU.subtract))
                link(v.scalar_tensor_tensor(rope_t, out[:], -C1, posf, ALU.mult, ALU.add))
                link(v.scalar_tensor_tensor(rope_t, out[:], -C2, rope_t, ALU.mult, ALU.add))
                link(v.scalar_tensor_tensor(rope_t, out[:], -C3, rope_t, ALU.mult, ALU.add))
                link(v.tensor_scalar(rope_t, rope_t, 2 * PI * quarter, None, ALU.add))
                last = v.tensor_scalar(out[:], rope_t, 3.141592, -3.141592, ALU.min, ALU.max)
                if quarter:
                    last.then_inc(angles_ready, 1)
                else:
                    link(last)

            dve.wait_ge(x_landed, 16)
            dve.wait_ge(r1_ready, 1)
            link(v.reciprocal(rms[:, T:2 * T], rms[:, 0:T]))
            link(v.tensor_tensor(hT, xT[:], rms[:, T:2 * T].unsqueeze(1).broadcast_to([P, KT, T]), ALU.mult))
            dve.wait_ge(small_landed, 16)
            dve.wait_ge(ada_turned, 1)
            link(v.tensor_tensor(mod[:, 0:16], ps[:, 1, :].rearrange("p (a c) -> p a c", c=WIN)[:, :, 0:1].rearrange("p a c -> p (a c)"), sm("b_ada", 0, 16), ALU.add))
            link(v.scalar_tensor_tensor(a12[:, 0, :], mod[:, 8:16], 1.0, sm("g1"), ALU.add, ALU.mult))
            for k in range(KT):
                v.tensor_scalar(hT[:, k, :], hT[:, k, :], a12[:, 0, k:k + 1], mod[:, k:k + 1], ALU.mult, ALU.add).then_inc(h_ready, 1)

            dve.wait_ge(lat_sq_ready, 1)
            v.tensor_scalar(k_r, ps[0:ROPE, 4, T:2 * T], sm("gk_rope", parts=ROPE), None, ALU.mult).then_inc(krope_ready, 1)
            dve.wait_ge(lat_rms_ready, 1)
            link(v.reciprocal(rms, rms))
            lat_ps = [ps[:, 1, 0:T], ps[:, 1, T:2 * T], ps[:, 2, 0:T], ps[:, 2, T:2 * T], ps[:, 4, 0:T]]
            for m in range(3):
                link(v.scalar_tensor_tensor(q_lat[:, m, :], lat_ps[m], sm("g_qa", m, 1), rms[:, 0:T], ALU.mult, ALU.mult))
            for m in range(2):
                link(v.scalar_tensor_tensor(kv_lat[:, m, :], lat_ps[3 + m], sm("g_kva", m, 1), rms[:, T:2 * T], ALU.mult, ALU.mult))
            dve.wait_ge(trig_ready, 1)
            dve.wait_ge(kswap_ready, 1)
            link(v.tensor_tensor(rope_t, ps[0:ROPE, 5, 0:T], sin_t[:], ALU.mult))
            link(v.tensor_tensor(k_rot[:], k_r, cos_t[:], ALU.mult))
            link(v.tensor_tensor(k_rot[:], k_rot[:], rope_t, ALU.add))
            v.tensor_tensor(stat[:, 15:16], sm("gq_nope"), sm("gk_nope"), ALU.mult).then_inc(lat_norm_ready, 1)

            for read_out in (kq_ready, merged_ready, u_done, max_ready, y_done):
                dve.sem_inc(read_out, 1)
            base, STEPS = chain[0], 14
            with dve.Fori(0, HEADS // 2) as i:
                for half in range(2):
                    n = i * 2 + (half + 1)
                    j = i * 2 + half
                    chain[0], chain[1] = base + half * STEPS, i * (2 * STEPS)
                    dve.wait_ge(sq_ready, n)
                    if half == 0:
                        dve.wait_ge(lat_norm_ready, 1)
                    v.tensor_scalar(q_x, ps[0:ROPE, 1, 0:T], sm("gq_rope", parts=ROPE), None, ALU.mult).then_inc(qx_ready, 1)
                    link(v.tensor_scalar(q_n, ps[:, 0, 0:T], stat[:, 15:16], None, ALU.mult))
                    dve.wait_ge(rk_sqrt, n)
                    link(v.reciprocal(rk, rk_s))
                    link(v.tensor_tensor(k_n, rk, ps[:, 0, T:2 * T], ALU.mult))
                    link(v.tensor_tensor(k_r, k_rot[:], rk[0:ROPE, :], ALU.mult))
                    dve.wait_ge(qx_ready, n)
                    link(v.tensor_tensor(q_r, q_x, cos_t[:], ALU.mult))
                    dve.wait_ge(swap_ready, n)
                    link(v.tensor_tensor(rope_t, sin_t[:], ps[0:ROPE, 1, T:2 * T], ALU.mult))
                    v.tensor_tensor(q_r, q_r, rope_t, ALU.add).then_inc(kq_ready, 1)
                    dve.wait_ge(zx_copied, n)
                    v.tensor_tensor(u[:, 2:T + 2], zx, ps[:, 5, T:2 * T], ALU.mult).then_inc(u_done, 1)
                    dve.wait_ge(u_done, n + 1)
                    c0 = SMALL["conv"][0]
                    link(v.tensor_scalar(conv_t, u[:, 0:T], small[:, bass.ds(j + c0, 1)], None, ALU.mult))
                    link(v.scalar_tensor_tensor(conv_t, u[:, 1:T + 1], small[:, bass.ds(j + (c0 + KT), 1)], conv_t, ALU.mult, ALU.add))
                    link(v.scalar_tensor_tensor(conv_t, u[:, 2:T + 2], small[:, bass.ds(j + (c0 + 2 * KT), 1)], conv_t, ALU.mult, ALU.add))
                    dve.wait_ge(qs_sqrt, n)
                    dve.wait_ge(s_ready, n)
                    v.reciprocal(stat[:, 2:4], stat[:, 0:2])
                    mask = co("mask")
                    v.tensor_tensor_reduce(out=scores[:, 0:P], in0=ps[:, 3, 0:P], in1=mask[:, P:T], scale=1.0, scalar=2 * LOW,
                                           op0=ALU.add, op1=ALU.max, accum_out=stat[:, 4:5])
                    link(v.tensor_tensor_reduce(out=scores[:, P:P + T], in0=ps[:, 3, P:P + T], in1=mask, scale=1.0, scalar=2 * LOW,
                                                op0=ALU.add, op1=ALU.max, accum_out=stat[:, 5:6]))
                    v.scalar_tensor_tensor(stat[:, 6:8], stat[:, 4:6], -1.0, stat[:, 2:4], ALU.mult, ALU.mult).then_inc(max_ready, 1)
                    dve.wait_ge(exp_done, n)
                    link(v.reciprocal(stat[:, 10:12], stat[:, 8:10]))
                    link(v.tensor_scalar(probs[:, 0:P], probs[:, 0:P], stat[:, 10:11], None, ALU.mult))
                    v.tensor_scalar(probs[:, P:P + T], probs[:, P:P + T], stat[:, 11:12], None, ALU.mult).then_inc(p_ready, 1)
                    dve.wait_ge(conv_gate_ready, n)
                    link(v.scalar_tensor_tensor(y_conv, ps[:, 6, 0:T], 0.5, conv_t, ALU.mult, ALU.mult))
                    v.scalar_tensor_tensor(y_conv, t_gate, 1.0, y_conv, ALU.add, ALU.mult).then_inc(y_done, 1)
                    dve.wait_ge(mla_gate_ready, n)
                    dve.wait_ge(o_ready, n)
                    dve.wait_ge(y_done, n + 1)
                    link(v.scalar_tensor_tensor(o_t, m_gate, 1.0, ps[:, 2, T:2 * T], ALU.add, ALU.mult))
                    v.scalar_tensor_tensor(merged[:, bass.ds(j, 1), :].rearrange("p a n -> p (a n)"), o_t, 0.5, y_conv, ALU.mult, ALU.add).then_inc(merged_ready, 1)
                    used = chain[0] - (base + half * STEPS)
                    assert used == STEPS, used
            chain[0], chain[1] = base + HEADS * STEPS, None

            for b2, bank in ((0, 7), (1, 0)):
                dve.wait_ge(ada_turned, b2 + 2)
                link(v.tensor_tensor(mod[:, 16 + 16 * b2:32 + 16 * b2], ps[:, bank, :].rearrange("p (a c) -> p a c", c=WIN)[:, :, 0:1].rearrange("p a c -> p (a c)"),
                                     sm("b_ada", 16 + 16 * b2, 16), ALU.add))
            link(v.scalar_tensor_tensor(a12[:, 1, :], mod[:, 32:40], 1.0, sm("g2"), ALU.add, ALU.mult))
            for a in range(2):
                dve.wait_ge(wo_ready, a + 1)
                for m in range(4):
                    last = v.scalar_tensor_tensor(xT[:, 4 * a + m, :], ps[:, 1 + 2 * a + m // 2, (m % 2) * T:(m % 2 + 1) * T],
                                                  mod[:, 16 + 4 * a + m:17 + 4 * a + m], xT[:, 4 * a + m, :], ALU.mult, ALU.add)
                last.then_inc(x2_ready, 1)
            dve.wait_ge(x2_ready, 2)
            dve.wait_ge(r2_ready, 1)
            link(v.reciprocal(r2, r2s))
            link(v.tensor_tensor(hT, xT[:], r2.unsqueeze(1).broadcast_to([P, KT, T]), ALU.mult))
            for k in range(KT):
                v.tensor_scalar(hT[:, k, :], hT[:, k, :], a12[:, 1, k:k + 1], mod[:, 24 + k:25 + k], ALU.mult, ALU.add).then_inc(h2_ready, 1)

            dve.wait_ge(lg_ready, 1)
            logits_ps = ps[:, 6, 0:128].rearrange("p (t n) -> p t n", t=TT)[:, :, 0:36]
            link(v.tensor_tensor(lg, logits_ps, sm("b_router").unsqueeze(1).broadcast_to([P, TT, 36]), ALU.add))
            G = [P, TT, GROUPS]
            E = [P, TT, PER_GROUP]
            G4 = [P, GROUPS, PER_GROUP]

            def b(ap, shape):
                return ap.unsqueeze(2).broadcast_to(shape)

            def first_of_max(values, number, top, tmp, onehot, shape, idx):
                link(v.tensor_reduce(top, values, AX_X, ALU.max))
                link(v.tensor_tensor(tmp, values, b(top, shape), ALU.is_equal))
                link(v.tensor_tensor(tmp, tmp, number, ALU.mult))
                link(v.tensor_reduce(idx, tmp, AX_X, ALU.min))
                link(v.tensor_tensor(onehot, number, b(idx, shape), ALU.is_equal))

            g_no = co("group_no").unsqueeze(1).broadcast_to(G)
            e_no = co("expert_no").unsqueeze(1).broadcast_to(E)
            lg_g = lg[:, :, 0:GROUPS]
            first_of_max(lg_g, g_no, s_work[:, 0, :], g_work[:, 0], g_work[:, 2], G, s_work[:, 1, :])
            v.tensor_tensor(g_work[:, 1], lg_g, b(s_work[:, 0, :], G), ALU.subtract).then_inc(gdiff_ready, 1)
            for t in range(TT):
                link(v.tensor_tensor(oh[:, 3, t, :].rearrange("p (g e) -> p g e", g=GROUPS),
                                     lg[:, t, GROUPS:].rearrange("p (g e) -> p g e", g=GROUPS),
                                     g_work[:, 2, t, :].unsqueeze(2).broadcast_to(G4), ALU.mult))
                link(v.tensor_reduce(e_work[:, 0, t, :], oh[:, 3, t, :].rearrange("p (g e) -> p e g", g=GROUPS), AX_X, ALU.add))
            first_of_max(e_work[:, 0], e_no, s_work[:, 2, :], e_work[:, 1], e_work[:, 2], E, s_work[:, 3, :])
            link(v.scalar_tensor_tensor(e_work[:, 3].rearrange("p t n -> p (t n)"), e_work[:, 2].rearrange("p t n -> p (t n)"), LOW,
                                        e_work[:, 0].rearrange("p t n -> p (t n)"), ALU.mult, ALU.add))
            first_of_max(e_work[:, 3], e_no, s_work[:, 4, :], e_work[:, 1], e_work[:, 4], E, s_work[:, 3, :])
            v.tensor_tensor(s_work[:, 5, :], s_work[:, 4, :], s_work[:, 2, :], ALU.subtract).then_inc(ediff_ready, 1)
            for c, e in ((0, 2), (1, 4)):
                for t in range(TT):
                    link(v.tensor_tensor(oh[:, c, t, :].rearrange("p (g e) -> p g e", g=GROUPS),
                                         g_work[:, 2, t, :].unsqueeze(2).broadcast_to(G4),
                                         e_work[:, e, t, :].unsqueeze(1).broadcast_to(G4), ALU.mult))
            v.tensor_tensor(oh[:, 2], oh[:, 0], oh[:, 1], ALU.add).then_inc(onehot_ready, 1)
            dve.wait_ge(gexp_ready, 1)
            link(v.tensor_reduce(s_work[:, 7, :], g_work[:, 1], AX_X, ALU.add))
            dve.wait_ge(eexp_ready, 1)
            link(v.scalar_tensor_tensor(s_work[:, 8, :], s_work[:, 6, :], 1.0, s_work[:, 7, :], ALU.add, ALU.mult))
            link(v.reciprocal(s_work[:, 8, :], s_work[:, 8, :]))
            link(v.tensor_tensor(s_work[:, 9, :], s_work[:, 8, :], s_work[:, 6, :], ALU.mult))
            dve.wait_ge(rank_ready, 1)
            link(v.tensor_copy(cnt, ps[:, 7, 64:96]))
            link(v.tensor_tensor_scan(incl, ones[:, 0:EXPERTS], cnt, 0.0, ALU.mult, ALU.add))
            link(v.tensor_tensor(offf, incl, cnt, ALU.subtract))
            link(v.tensor_scalar(wins[:, 0:EXPERTS], cnt, 1.0, 1.0 / WIN, ALU.max, ALU.mult))
            link(v.tensor_scalar(wins[:, 0:EXPERTS], wins[:, 0:EXPERTS], 0.5 - 0.5 / WIN, MAGIC, ALU.add, ALU.add))
            link(v.tensor_scalar(wins[:, 0:EXPERTS], wins[:, 0:EXPERTS], MAGIC, None, ALU.subtract))
            link(v.tensor_tensor_scan(wins[:, 2 * EXPERTS:], ones[:, 0:EXPERTS], wins[:, 0:EXPERTS], 0.0, ALU.mult, ALU.add))
            link(v.tensor_tensor(wins[:, EXPERTS:2 * EXPERTS], wins[:, 2 * EXPERTS:], wins[:, 0:EXPERTS], ALU.subtract))
            v.tensor_copy(table[0:1, 0:EXPERTS], offf[0:1, :])
            v.tensor_copy(table[0:1, EXPERTS:], wins[0:1, EXPERTS:]).then_inc(table_ready, 1)
            link(v.tensor_tensor(pos_e, ps[:, 7, 0:64].rearrange("p (t n) -> p t n", t=TT), offf.unsqueeze(1).broadcast_to([P, TT, EXPERTS]), ALU.add))
            for c in range(2):
                link(v.tensor_tensor(oh[:, 3], oh[:, c], pos_e, ALU.mult))
                link(v.tensor_reduce(s_work[:, 10 + c, :], oh[:, 3], AX_X, ALU.add))
            slot_no = co("slot_no")
            for t in range(TT):
                link(v.tensor_scalar(sel[:, t, :], slot_no, s_work[:, 10, t:t + 1], None, ALU.is_equal))
                v.scalar_tensor_tensor(sel[:, t, :], slot_no, s_work[:, 11, t:t + 1], sel[:, t, :], ALU.is_equal, ALU.add).then_inc(sel_ready, 1)
            for t in range(TT):
                link(v.tensor_scalar(sel_w[:, t, :], slot_no, s_work[:, 10, t:t + 1], s_work[:, 8, t:t + 1], ALU.is_equal, ALU.mult))
                link(v.tensor_scalar(comb_t, slot_no, s_work[:, 11, t:t + 1], s_work[:, 9, t:t + 1], ALU.is_equal, ALU.mult))
                v.tensor_tensor(sel_w[:, t, :], sel_w[:, t, :], comb_t, ALU.add).then_inc(comb_rows_ready, 1)
            for k in range(1, KT, 2):
                dve.wait_ge(xg_ready, k + 1)
                v.tensor_copy(xg[:, k, 0:SLOTS], ps[:, k, :]).then_inc(xg_dve, 1)

            dve.wait_ge(table_ready, 1)
            with dve.Fori(0, EXPERTS) as e:
                off, at, upto = window_table(dve, e)
                with dve.Fori(0, upto - at) as w:
                    n = at + w + 1
                    dve.wait_ge(silu_done, n)
                    v.tensor_tensor(act_t, silu_t, ps[:, 1, 2 * WIN:4 * WIN], ALU.mult).then_inc(act_done, 1)
                    dve.wait_ge(down_ready, n)
                    v.tensor_copy(d_sb, ps[:, 2, 0:T]).then_inc(down_copied, 1)
            for m in range(KT):
                dve.wait_ge(out_ready, m + 1)
                v.scalar_tensor_tensor(xT[:, m, :], ps[:, 4 + m % 4, 0:T], mod[:, 40 + m:41 + m], xT[:, m, :], ALU.mult, ALU.add).then_inc(out_done, 1)


def constants():
    import numpy as np
    c = np.zeros((P, N_CONST), np.float32)

    def put(name, a):
        at, w = CONST[name]
        c[0:a.shape[0], at:at + w] = a

    put("ident", np.eye(P, dtype=np.float32))
    r = np.arange(P)
    put("before", (r[:, None] < r[None, :]).astype(np.float32))
    swap = np.zeros((ROPE, ROPE), np.float32)
    h = ROPE // 2
    for m in range(h):
        swap[m + h, m] = -1.0
        swap[m, m + h] = 1.0
    put("swap", np.concatenate([swap, swap], axis=1))
    put("slot_no", np.broadcast_to(np.arange(SLOTS, dtype=np.float32), (P, SLOTS)))
    mask = np.zeros((P, T), np.float32)
    mask[0:CHUNK, T - CHUNK:] = LOW
    put("mask", mask)
    put("group_no", np.broadcast_to(np.arange(GROUPS, dtype=np.float32) - 100, (P, GROUPS)))
    put("expert_no", np.broadcast_to(np.arange(PER_GROUP, dtype=np.float32) - 100, (P, PER_GROUP)))
    inv = np.float32(10000.0) ** (-np.arange(0, ROPE, 2, dtype=np.float32) / np.float32(ROPE))
    put("inv_freq", np.concatenate([inv, inv]).astype(np.float32)[:, None])
    return c


def kernel(**inputs):
    import numpy as np
    import concourse.bacc as bacc
    from concourse.bass_utils import run_bass_kernel_spmd as run

    a = {k: np.asarray(v) for k, v in inputs.items()}

    def cols(x):
        return x.reshape(-1, P).T

    def tiles(w, m):
        return w.reshape(w.shape[0] // P, P, m, P).transpose(1, 2, 0, 3).reshape(P, -1)

    def kcols(w):
        return w.reshape(w.shape[0] // P, P, -1).transpose(1, 0, 2).reshape(P, -1)

    small = np.zeros((P, N_SMALL), np.float32)

    def put(name, x):
        at, w = SMALL[name]
        small[0:x.shape[0], at:at + w] = x

    put("b_ada", cols(a["b_ada"][0]))
    put("g1", cols(a["norm1_g"][0]))
    put("g2", cols(a["norm2_g"][0]))
    put("c", cols(a["c"][0]))
    put("g_qa", cols(a["q_a_norm_g"][0]))
    put("g_kva", cols(a["kv_a_norm_g"][0]))
    put("gq_nope", a["q_norm_g"][0, :NOPE, None])
    put("gk_nope", a["k_norm_g"][0, :NOPE, None])
    put("gq_rope", a["q_norm_g"][0, NOPE:, None])
    put("gk_rope", a["k_norm_g"][0, NOPE:, None])
    put("conv", a["conv_w"][0].reshape(3 * KT, P).T)
    put("b_router", np.broadcast_to(np.concatenate([a["b_router_group"][0], a["b_router_expert"][0]]), (P, 36)))
    put("w_router", kcols(np.concatenate([a["w_router_group"][0], a["w_router_expert"][0]], axis=1)))

    w_in = a["w_in"][0]
    lat0 = 3 * D
    rope0 = lat0 + QL + KVL
    gc0 = rope0 + ROPE
    lat = np.concatenate([tiles(w_in[:, lat0:rope0], LAT_TILES), kcols(w_in[:, rope0:gc0])], axis=1)
    mix = []
    for j in range(HEADS):
        parts = [tiles(w_in[:, o + j * P:o + (j + 1) * P], 1) for o in (0, 2 * D, D, gc0, gc0 + D)]
        parts.append(kcols(a["w_q_b"][0][:, j * QK:(j + 1) * QK]))
        parts.append(kcols(a["w_kv_b"][0][:, j * 256:(j + 1) * 256]))
        mix.append(np.concatenate(parts, axis=1))
    wa = a["w_ada"][0]
    ada = np.stack([kcols(wa[:, n * 512:(n + 1) * 512]) for n in range(ADA_ITEMS)])
    wo = np.stack([tiles(a["w_o"][0][:, n * 512:(n + 1) * 512], 4) for n in range(2)])
    gate = a["w_exp_gate"][0].reshape(EXPERTS, KT, P, FF)
    up = a["w_exp_up"][0].reshape(EXPERTS, KT, P, FF)
    gate_up = np.concatenate([gate, up], axis=3).transpose(0, 2, 1, 3).reshape(EXPERTS, P, -1)
    down = a["w_exp_down"][0].reshape(EXPERTS, FF // P, P, D).transpose(0, 2, 1, 3).reshape(EXPERTS, P, -1)
    arrays = {
        "xT": a["x"][0].T.reshape(KT, P, T).transpose(1, 0, 2),
        "pos": np.broadcast_to(a["positions"], (ROPE, T)),
        "small": small,
        "const": constants(),
        "ada": ada,
        "lat": lat,
        "mix": np.stack(mix),
        "wo": wo,
        "gu": gate_up,
        "down": down,
    }
    arrays = {"in_" + k: np.ascontiguousarray(v) for k, v in arrays.items()}
    nc = bacc.Bacc("TRN2", target_bir_lowering=False, num_devices=1)
    aps = [nc.dram_tensor(k, v.shape, mybir.dt.from_np(v.dtype), kind="ExternalInput").ap() for k, v in arrays.items()]
    out = nc.dram_tensor("out_yT", (KT, P, T), F32, kind="ExternalOutput").ap()
    block_kernel(nc, *aps, out)
    r = run(nc, [arrays], core_ids=[0])
    y = np.asarray(r.results[0]["out_yT"])
    return np.ascontiguousarray(y.reshape(D, T).T).reshape(1, T, D)
```

```python
from contextlib import ExitStack

import concourse.bass as bass
from concourse import mybir

F32 = mybir.dt.float32
I32 = mybir.dt.int32
ACT = mybir.ActivationFunctionType
ALU = mybir.AluOpType
AX_X = mybir.AxisListType.X
PI = 3.14159265358979

P = 128
D = 1024
T = 256
KT = D // P
TT = T // P
HEADS = 8
NOPE, ROPE = 128, 64
QK = NOPE + ROPE
QL, KVL = 384, 256
GROUPS, PER_GROUP = 4, 8
EXPERTS = GROUPS * PER_GROUP
FF = 256
SLOTS = 2 * T
WIN = 32
EPS = 1e-6
LOW = -1.0e30
CHUNK = 64

SMALL_WIDTHS = (("b_ada", 48), ("g1", KT), ("g2", KT), ("c", KT), ("g_qa", 3), ("g_kva", 2),
                ("gq_nope", 1), ("gk_nope", 1), ("gq_rope", 1), ("gk_rope", 1), ("conv", 3 * KT),
                ("b_router", 36), ("w_router", KT * 36))
CONST_WIDTHS = (("ident", P), ("before", P), ("swap", P), ("slot_no", SLOTS + WIN), ("mask", T),
                ("group_no", GROUPS), ("expert_no", PER_GROUP), ("inv_freq", 1), ("row_no", 1))


def places(widths):
    at, out = 0, {}
    for name, width in widths:
        out[name] = (at, width)
        at += width
    return out, at


SMALL, N_SMALL = places(SMALL_WIDTHS)
CONST, N_CONST = places(CONST_WIDTHS)

ADA_ITEMS, ADA_TILES = 12, 4
ADA_COLS = KT * ADA_TILES * P
LAT_TILES = 5
LAT_COLS = KT * (LAT_TILES * P + ROPE)
CONV_COLS = KT * 5 * P
WQ_AT = CONV_COLS
WKV_AT = WQ_AT + 3 * QK
MIX_COLS = WKV_AT + 2 * 256
WO_COLS = KT * 4 * P
GU_COLS = 2 * KT * FF
DOWN_COLS = (FF // P) * D
EX_SLOTS = 5
OWN = 4
WINDOWS = EXPERTS + SLOTS // WIN
NW = WINDOWS + 1
SELW = SLOTS + WIN


def block_kernel(nc, xT_d, pos_d, small_d, const_d, ada_d, lat_d, mix_d, wo_d, gu_d, down_d, out_d):
    with ExitStack() as ctx:
        def sb(name, shape, dt=F32):
            return ctx.enter_context(nc.sbuf_tensor(name, shape, dt))

        def sem(name):
            return ctx.enter_context(nc.semaphore(name))

        ps = ctx.enter_context(nc.psum_tensor("ps", [P, 8, 512], F32))

        wex = sb("wex", [P, OWN, GU_COLS + DOWN_COLS])
        wmix = sb("wmix", [P, 2, MIX_COLS])
        ex_place = [wex[:, s, :] for s in range(OWN)] + [wmix[:, 1, 0:GU_COLS + DOWN_COLS]]
        yT = wmix[:, 0, 0:KT * SELW].rearrange("p (k s) -> p k s", k=KT)
        xT = sb("xT", [P, KT, T])
        act2 = sb("act2", [P, 2 * KT, T])
        hT = act2[:, 0:KT, :]
        merged = act2[:, KT:2 * KT, :]
        h2_rows = merged.rearrange("p (t a) n -> p t (a n)", t=TT)
        diag = hT.rearrange("p (a k) n -> p a (k n)", a=2)[:, 0, :].rearrange("p (a t n) -> p a t n", a=4, t=TT)
        y_rows = hT.rearrange("p k n -> p (k n)")
        small = sb("small", [P, N_SMALL])
        const = sb("const", [P, N_CONST])
        ones = sb("ones", [P, P])
        eps_q = sb("eps_q", [P, 1])
        eps_1 = sb("eps_1", [P, 1])
        c_rep = sb("c_rep", [P, KT, WIN])
        mod = sb("mod", [P, 48])
        a12 = sb("a12", [P, 2, KT])
        cos_t = sb("cos_t", [ROPE, T])
        sin_t = sb("sin_t", [ROPE, T])
        k_rot = sb("k_rot", [ROPE, T])
        k_rope_sq = sb("k_rope_sq", [ROPE, T])
        work = sb("work", [P, 6850])
        work_at = [0]

        def piece(cols, parts=P):
            a = work_at[0]
            work_at[0] += cols
            assert work_at[0] <= 6850
            return work[0:parts, a:a + cols]

        q_lat = piece(3 * T).rearrange("p (k n) -> p k n", k=3)
        kv_lat = piece(2 * T).rearrange("p (k n) -> p k n", k=2)
        q_sq = piece(T)
        k_sq = piece(T)
        q_n = piece(T)
        q_x = piece(T, ROPE)
        q_r = piece(T, ROPE)
        rope_t = piece(T, ROPE)
        qr_sq = rope_t
        k_n = piece(T)
        k_r = piece(T, ROPE)
        v_sb = piece(2 * P).rearrange("p (a b) -> p a b", a=2)
        rms = piece(2 * T)
        rk_s, rk = rms[:, 0:T], rms[:, T:2 * T]
        scores = piece(P + T)
        probs = piece(P + T)
        pT = piece(P + T)
        zx = piece(T)
        t_gate = piece(T)
        m_gate = piece(T)
        conv_t = piece(T)
        y_conv = piece(T)
        o_t = zx
        u = piece(T + 2)
        stat = piece(16)
        posi, posf = q_x.bitcast(I32), k_r
        work_at[0] = 0
        sel = piece(TT * SELW).rearrange("p (t s) -> p t s", t=TT)
        spread = piece(4 * T).rearrange("p (a n) -> p a n", a=4)
        sel_win = piece(TT * WIN).rearrange("p (t n) -> p t n", t=TT)
        rows_sb = piece(T)
        xw = piece(KT * WIN).rearrange("p (k n) -> p k n", k=KT)
        gu_sb = piece(P)
        silu_t = piece(2 * WIN)
        act_t = piece(2 * WIN)
        d_sb = piece(T)
        comb = piece(4 * T).rearrange("p (s n) -> p s n", s=4)
        comb_b = piece(T)
        diag_win = piece(P)
        wins = piece(6 * EXPERTS)
        lg = piece(72).rearrange("p (t n) -> p t n", t=TT)
        r2s = piece(T)
        r2 = piece(T)
        g_work = piece(5 * 8).rearrange("p (a t n) -> p a t n", a=5, t=TT)
        e_work = piece(6 * 16).rearrange("p (a t n) -> p a t n", a=6, t=TT)
        s_work = piece(24).rearrange("p (a t) -> p a t", a=12)
        oh = piece(4 * 64).rearrange("p (a t n) -> p a t n", a=4, t=TT)
        pos_e = piece(64).rearrange("p (t n) -> p t n", t=TT)
        cnt = piece(EXPERTS)
        incl = piece(EXPERTS)
        offf = piece(EXPERTS)
        table = sb("table", [1, EXPERTS + 1 + NW], I32)
        ada_beside = wex[:, OWN - 1, 0:ADA_COLS]
        ada_rows = wex[:, OWN - 1, GU_COLS:GU_COLS + P]

        def sm(name, i=0, n=None, parts=P):
            a, w = SMALL[name]
            return small[0:parts, a + i:a + i + (n or w)]

        def co(name, parts=P):
            a, w = CONST[name]
            return const[0:parts, a:a + w]

        ident, before = co("ident"), co("before")

        x_landed, small_landed, const_landed, pos_landed = sem("x_landed"), sem("small_landed"), sem("const_landed"), sem("pos_landed")
        mix_landed = [sem("mix_landed0"), sem("mix_landed1")]
        ada_landed = [sem(f"ada_landed{s}") for s in range(4)]
        ada_done = sem("ada_done")
        gu_landed = [sem(f"gu_landed{s}") for s in range(EX_SLOTS)]
        down_landed = [sem(f"down_landed{s}") for s in range(EX_SLOTS)]
        dve_step = sem("dve_step")
        setup_done = sem("setup_done")
        c_ready, xsq_ready, xss_ready, r1_ready = sem("c_ready"), sem("xsq_ready"), sem("xss_ready"), sem("r1_ready")
        h_ready = sem("h_ready")
        lat_ready, lat_sq_ready, lat_ss_ready, lat_rms_ready = sem("lat_ready"), sem("lat_sq_ready"), sem("lat_ss_ready"), sem("lat_rms_ready")
        angles_ready, trig_ready = sem("angles_ready"), sem("trig_ready")
        krope_ready, kswap_ready, lat_norm_ready = sem("krope_ready"), sem("kswap_ready"), sem("lat_norm_ready")
        qk_ready, qr_ready, v_ready = sem("qk_ready"), sem("qr_ready"), sem("v_ready")
        sq_ready, v_copied, qx_ready = sem("sq_ready"), sem("v_copied"), sem("qx_ready")
        kss_ready, qss_ready, swap_ready = sem("kss_ready"), sem("qss_ready"), sem("swap_ready")
        rk_sqrt, qs_sqrt, kq_ready = sem("rk_sqrt"), sem("qs_sqrt"), sem("kq_ready")
        zxc_ready, zx_copied, u_done = sem("zxc_ready"), sem("zx_copied"), sem("u_done")
        s_ready, max_ready, exp_done, p_ready = sem("s_ready"), sem("max_ready"), sem("exp_done"), sem("p_ready")
        zbg_ready, conv_gate_ready, y_done = sem("zbg_ready"), sem("conv_gate_ready"), sem("y_done")
        pT_ready, pT_copied = sem("pT_ready"), sem("pT_copied")
        zgm_ready, mla_gate_ready = sem("zgm_ready"), sem("mla_gate_ready")
        o_ready, merged_ready = sem("o_ready"), sem("merged_ready")
        wo_ready, x2_ready, x2sq_ready, x2ss_ready, r2_ready, h2_ready = (sem("wo_ready"), sem("x2_ready"), sem("x2sq_ready"), sem("x2ss_ready"), sem("r2_ready"), sem("h2_ready"))
        h2_scaled = sem("h2_scaled")
        lg_ready, h2r_ready, h2r_copied = sem("lg_ready"), sem("h2r_ready"), sem("h2r_copied")
        gdiff_ready, gexp_ready, ediff_ready, eexp_ready = sem("gdiff_ready"), sem("gexp_ready"), sem("ediff_ready"), sem("eexp_ready")
        onehot_ready, rank_ready, table_ready, sel_ready = (sem("onehot_ready"), sem("rank_ready"), sem("table_ready"), sem("sel_ready"))
        wslot_ready, wrow_ready = sem("wslot_ready"), sem("wrow_ready")
        diag_ready, spread_ready, spread_copied = sem("diag_ready"), sem("spread_ready"), sem("spread_copied")
        ada_copied, ada_turned = sem("ada_copied"), sem("ada_turned")
        mod_ready = sem("mod_ready")
        xw_ready, gu_ready, gu_copied, gu_turned = sem("xw_ready"), sem("gu_ready"), sem("gu_copied"), sem("gu_turned")
        silu_done, act_done, down_ready, down_copied = sem("silu_done"), sem("act_done"), sem("down_ready"), sem("down_copied")
        sel_win_ready, rows_ready, rows_copied, rows_turned = sem("sel_win_ready"), sem("rows_ready"), sem("rows_copied"), sem("rows_turned")
        down_turned, y_stored, comb_ready = sem("down_turned"), sem("y_stored"), sem("comb_ready")
        yr_ready, yr_copied, out_ready, out_done, out_stored = (sem("yr_ready"), sem("yr_copied"), sem("out_ready"), sem("out_done"), sem("out_stored"))

        MIX0 = 1
        WO0 = MIX0 + HEADS
        block = ctx.enter_context(nc.Block())

        def windows_before(eng, e):
            return eng.value_load(table[0:1, bass.ds(e, 1)], min_val=0, max_val=WINDOWS)

        def window_slot(eng, n):
            return eng.value_load(table[0:1, bass.ds(n + (EXPERTS + 1), 1)], min_val=0, max_val=SLOTS)

        @block.sync
        def _(sp):
            sp.dma_start(small[:], small_d).then_inc(small_landed, 16)

            def ada_load(n):
                sp.dma_start(wex[:, n, 0:ADA_COLS], ada_d[n]).then_inc(ada_landed[n], 16)

            def expert_load(s):
                sp.dma_start(ex_place[s][:, 0:GU_COLS], gu_d[s]).then_inc(gu_landed[s], 16)
                sp.dma_start(ex_place[s][:, GU_COLS:], down_d[s]).then_inc(down_landed[s], 16)

            def ring(n, dst_cols, src):
                before_it = n - 2
                if before_it == 0:
                    sp.wait_ge(lat_ready, 1)
                elif before_it >= MIX0:
                    sp.wait_ge(zgm_ready, before_it - MIX0 + 1)
                sp.dma_start(wmix[:, n % 2, 0:dst_cols], src).then_inc(mix_landed[n % 2], 16)

            ada_load(0)
            sp.dma_start(xT[:], xT_d).then_inc(x_landed, 16)
            sp.dma_start(const[:], const_d).then_inc(const_landed, 16)
            sp.dma_start(posi, pos_d).then_inc(pos_landed, 16)
            for n in range(1, 4):
                ada_load(n)
            ring(0, LAT_COLS, lat_d)
            for j in range(HEADS):
                ring(MIX0 + j, MIX_COLS, mix_d[j])
                sp.wait_ge(ada_done, 4 + j)
                sp.dma_start(ada_beside, ada_d[4 + j]).then_inc(ada_landed[3], 16)
                if 1 <= j < OWN:
                    expert_load(j - 1)
            for n in range(2):
                ring(WO0 + n, WO_COLS, wo_d[n])
            sp.wait_ge(ada_turned, 1 + HEADS)
            expert_load(OWN - 1)
            sp.wait_ge(wo_ready, 1)
            expert_load(OWN)
            sp.wait_ge(table_ready, 1)

            def next_expert(s, e):
                upto = windows_before(sp, e + 1)
                sp.wait_ge(gu_ready, upto)
                sp.dma_start(ex_place[s][:, 0:GU_COLS], gu_d[bass.ds(e + EX_SLOTS, 1)].rearrange("a p c -> p (a c)")).then_inc(gu_landed[s], 16)
                sp.wait_ge(down_ready, upto)
                sp.dma_start(ex_place[s][:, GU_COLS:], down_d[bass.ds(e + EX_SLOTS, 1)].rearrange("a p c -> p (a c)")).then_inc(down_landed[s], 16)

            with sp.Fori(0, EXPERTS // EX_SLOTS - 1) as i:
                for s in range(EX_SLOTS):
                    next_expert(s, i * EX_SLOTS + s)
            for s in range(EXPERTS % EX_SLOTS):
                next_expert(s, EXPERTS - EXPERTS % EX_SLOTS - EX_SLOTS + s)
            for m in range(KT):
                sp.wait_ge(out_done, m + 1)
                sp.dma_start(out_d[m], xT[:, m, :]).then_inc(out_stored, 16)
            sp.wait_ge(out_stored, 16 * KT)

        @block.gpsimd
        def _(pool):
            pool.wait_ge(table_ready, 1)
            pool.wait_ge(sel_ready, 2)
            pool.sem_inc(rows_ready, 1)
            with pool.Fori(0, windows_before(pool, EXPERTS) + 1) as n:
                at = window_slot(pool, n)
                pool.wait_ge(rows_ready, n + 1)
                nc.gpsimd.tensor_copy(sel_win, sel[:, :, bass.ds(at, WIN)]).then_inc(sel_win_ready, 1)

        @block.scalar
        def _(act):
            act.wait_ge(small_landed, 16)
            nc.scalar.activation(c_rep[:], sm("c").unsqueeze(2).broadcast_to([P, KT, WIN]), ACT.Silu).then_inc(c_ready, 1)
            act.wait_ge(x_landed, 16)
            nc.scalar.activation(merged, xT[:], ACT.Square).then_inc(xsq_ready, 1)
            act.wait_ge(angles_ready, 1)
            nc.scalar.activation(sin_t[:], sin_t[:], ACT.Sin)
            nc.scalar.activation(cos_t[:], cos_t[:], ACT.Sin).then_inc(trig_ready, 1)
            act.wait_ge(xss_ready, 1)
            act.wait_ge(setup_done, 4)
            nc.scalar.activation(rms[:, 0:T], ps[:, 3, 0:T], ACT.Sqrt, bias=eps_1[:], scale=1.0 / D).then_inc(r1_ready, 1)

            act.wait_ge(ada_done, 4)
            nc.scalar.copy(act2[:, 8:10, :].rearrange("p a n -> p (a n)"), ps[:, 0, :]).then_inc(ada_copied, 1)

            act.wait_ge(lat_ready, 1)
            nc.scalar.activation(merged[:, 0:2, :], ps[:, 1, :], ACT.Square)
            nc.scalar.activation(merged[:, 2:4, :], ps[:, 2, :], ACT.Square)
            nc.scalar.activation(merged[:, 4, :], ps[:, 4, 0:T], ACT.Square)
            nc.scalar.activation(k_rope_sq[:], ps[0:ROPE, 4, T:2 * T], ACT.Square).then_inc(lat_sq_ready, 1)
            act.wait_ge(lat_ss_ready, 1)
            nc.scalar.activation(rms[:, 0:T], ps[:, 3, 0:T], ACT.Sqrt, bias=eps_1[:], scale=1.0 / QL)
            nc.scalar.activation(rms[:, T:2 * T], ps[:, 3, T:2 * T], ACT.Sqrt, bias=eps_1[:], scale=1.0 / KVL).then_inc(lat_rms_ready, 1)

            with act.Fori(0, HEADS // 2) as i:
                for half in range(2):
                    n = i * 2 + (half + 1)
                    act.wait_ge(qk_ready, n)
                    nc.scalar.activation(q_sq, ps[:, 0, 0:T], ACT.Square)
                    nc.scalar.activation(k_sq, ps[:, 0, T:2 * T], ACT.Square)
                    act.wait_ge(qr_ready, n)
                    nc.scalar.activation(qr_sq, ps[0:ROPE, 1, 0:T], ACT.Square).then_inc(sq_ready, 1)
                    act.wait_ge(v_ready, n)
                    nc.scalar.copy(v_sb, ps[:, 2, 0:2 * P].rearrange("p (a b) -> p a b", a=2)).then_inc(v_copied, 1)
                    act.wait_ge(kss_ready, n)
                    nc.scalar.activation(rk_s, ps[:, 3, 0:T], ACT.Sqrt, bias=eps_1[:], scale=1.0 / QK).then_inc(rk_sqrt, 1)
                    act.wait_ge(qss_ready, n)
                    nc.scalar.activation(stat[:, 0:2], ps[:, 4, 0:2], ACT.Sqrt, bias=eps_q[:], scale=1.0).then_inc(qs_sqrt, 1)
                    act.wait_ge(zxc_ready, n)
                    nc.scalar.copy(zx, ps[:, 5, 0:T]).then_inc(zx_copied, 1)
                    act.wait_ge(max_ready, n + 1)
                    nc.scalar.activation(probs[:, 0:P], scores[:, 0:P], ACT.Exp, bias=stat[:, 6:7], scale=stat[:, 2:3], accum_out=stat[:, 8:9])
                    nc.scalar.activation(probs[:, P:P + T], scores[:, P:P + T], ACT.Exp, bias=stat[:, 7:8], scale=stat[:, 3:4], accum_out=stat[:, 9:10]).then_inc(exp_done, 1)
                    act.wait_ge(ada_done, n + 4)
                    nc.scalar.copy(ada_rows, ps[:, 0, 0:P]).then_inc(ada_copied, 1)
                    act.wait_ge(zbg_ready, n)
                    nc.scalar.activation(t_gate, ps[:, 6, T:2 * T], ACT.Tanh, scale=0.5).then_inc(conv_gate_ready, 1)
                    act.wait_ge(pT_ready, n)
                    nc.scalar.copy(pT, ps[:, 4, 0:P + T]).then_inc(pT_copied, 1)
                    act.wait_ge(zgm_ready, n)
                    nc.scalar.activation(m_gate, ps[:, 7, 0:T], ACT.Tanh, scale=0.5).then_inc(mla_gate_ready, 1)

            for a in range(2):
                act.wait_ge(x2_ready, a + 1)
                nc.scalar.activation(hT[:, 4 * a:4 * a + 4, :], xT[:, 4 * a:4 * a + 4, :], ACT.Square).then_inc(x2sq_ready, 1)
            act.wait_ge(x2ss_ready, 1)
            nc.scalar.activation(r2s, ps[:, 5, 0:T], ACT.Sqrt, bias=eps_1[:], scale=1.0 / D).then_inc(r2_ready, 1)
            for k in range(KT):
                act.wait_ge(h2_scaled, k + 1)
                nc.scalar.activation(hT[:, k, :], hT[:, k, :], ACT.Identity, bias=mod[:, 24 + k:25 + k]).then_inc(h2_ready, 1)
            for b in range(4):
                act.wait_ge(h2r_ready, b + 1)
                nc.scalar.copy(h2_rows[:, b // 2, (b % 2) * 512:(b % 2) * 512 + 512], ps[:, 1 + b, :]).then_inc(h2r_copied, 1)
                if b == 1:
                    act.wait_ge(gdiff_ready, 1)
                    nc.scalar.activation(g_work[:, 1], g_work[:, 1], ACT.Exp).then_inc(gexp_ready, 1)
            act.wait_ge(ediff_ready, 1)
            nc.scalar.activation(s_work[:, 6, :], s_work[:, 5, :], ACT.Exp).then_inc(eexp_ready, 1)
            act.wait_ge(spread_ready, 1)
            nc.scalar.copy(spread, ps[:, 4:6, :].rearrange("p b (a n) -> p (b a) n", a=2)).then_inc(spread_copied, 1)

            act.wait_ge(table_ready, 1)
            act.sem_inc(y_stored, 1)
            with act.Fori(0, windows_before(act, EXPERTS)) as n:
                act.wait_ge(gu_turned, n + 1)
                nc.scalar.activation(silu_t, ps[:, 1, 0:2 * WIN], ACT.Silu).then_inc(silu_done, 1)
                act.wait_ge(down_ready, n + 1)
                nc.scalar.copy(d_sb, ps[:, 2, 0:T]).then_inc(down_copied, 1)
                at = window_slot(act, n)
                act.wait_ge(down_turned, n + 1)
                nc.scalar.copy(yT.rearrange("p (c h) s -> p c h s", c=4)[:, :, :, bass.ds(at, WIN)],
                               ps[:, 4, 0:2 * P].rearrange("p (h c n) -> p c h n", h=2, c=4)).then_inc(y_stored, 1)
            for m in range(KT):
                act.wait_ge(yr_ready, m + 1)
                nc.scalar.copy(y_rows[:, (m % 2) * 512:(m % 2) * 512 + 512], ps[:, m % 2, :]).then_inc(yr_copied, 1)

        @block.tensor
        def _(pe):
            def mm(out, lhsT, rhs, start, stop, **kw):
                return nc.tensor.matmul(out, lhsT, rhs, start=start, stop=stop, **kw)

            def ada_item(items, out):
                w = items.rearrange("p (k c) -> p k c", k=KT)
                for k in range(KT):
                    for q in range(4):
                        last = mm(out[q * WIN:(q + 1) * WIN, :], c_rep[:, k, :], w[:, k, q * P:(q + 1) * P], k == 0, k == KT - 1)
                return last

            pe.wait_ge(c_ready, 1)
            for n in range(4):
                pe.wait_ge(ada_landed[n], 16)
                ada_item(wex[:, n, 0:ADA_COLS], ps[:, 0, n * P:(n + 1) * P]).then_inc(ada_done, 1)
                if n == 0:
                    pe.wait_ge(setup_done, 4)
                    pe.wait_ge(xsq_ready, 1)
                    for k in range(KT):
                        last = mm(ps[:, 3, 0:T], ones[:], merged[:, k, :], k == 0, k == KT - 1)
                    last.then_inc(xss_ready, 1)
            pe.wait_ge(ada_copied, 1)
            pe.wait_ge(const_landed, 16)
            rows = act2[:, 8:10, :].rearrange("p a n -> p (a n)")
            for a in range(4):
                last = nc.tensor.transpose(ps[:, 1, a * P:(a + 1) * P], rows[:, a * P:(a + 1) * P], ident)
            last.then_inc(ada_turned, 1)

            pe.wait_ge(mix_landed[0], 16)
            pe.wait_ge(h_ready, KT)
            w = wmix[:, 0, 0:KT * LAT_TILES * P].rearrange("p (m k c) -> p m k c", m=LAT_TILES, k=KT)
            wr = wmix[:, 0, KT * LAT_TILES * P:LAT_COLS].rearrange("p (k c) -> p k c", k=KT)
            lat_ps = [ps[:, 1, 0:T], ps[:, 1, T:2 * T], ps[:, 2, 0:T], ps[:, 2, T:2 * T], ps[:, 4, 0:T]]
            for m in range(LAT_TILES):
                for k in range(KT):
                    mm(lat_ps[m], w[:, m, k, :], hT[:, k, :], k == 0, k == KT - 1)
            for k in range(KT):
                last = mm(ps[0:ROPE, 4, T:2 * T], wr[:, k, :], hT[:, k, :], k == 0, k == KT - 1)
            last.then_inc(lat_ready, 1)
            pe.wait_ge(lat_sq_ready, 1)
            for k in range(3):
                mm(ps[:, 3, 0:T], ones[:], merged[:, k, :], k == 0, k == 2)
            for k in range(2):
                last = mm(ps[:, 3, T:2 * T], ones[:], merged[:, 3 + k, :], k == 0, k == 1)
            last.then_inc(lat_ss_ready, 1)
            pe.wait_ge(krope_ready, 1)
            mm(ps[:, 5, 0:T], co("swap", ROPE), k_r, True, True).then_inc(kswap_ready, 1)
            pe.wait_ge(lat_norm_ready, 1)

            with pe.Fori(0, HEADS // 2) as i:
                for half in range(2):
                    done = i * 2 + half
                    slot = (MIX0 + half) % 2
                    w = wmix[:, slot, 0:CONV_COLS].rearrange("p (m k c) -> p m k c", m=5, k=KT)
                    wq = wmix[:, slot, WQ_AT:WKV_AT].rearrange("p (k c) -> p k c", k=3)
                    wkv = wmix[:, slot, WKV_AT:MIX_COLS].rearrange("p (k c) -> p k c", k=2)

                    def conv_tile(m, out):
                        for k in range(KT):
                            last = mm(out, w[:, m, k, :], hT[:, k, :], k == 0, k == KT - 1)
                        return last

                    pe.wait_ge(mix_landed[slot], i * 16 + 16 * ((MIX0 + half) // 2 + 1))
                    pe.wait_ge(kq_ready, done + 1)
                    pe.wait_ge(mod_ready, done + 1)
                    for k in range(3):
                        mm(ps[:, 0, 0:T], wq[:, k, 0:NOPE], q_lat[:, k, :], k == 0, k == 2)
                    for k in range(2):
                        last = mm(ps[:, 0, T:2 * T], wkv[:, k, 0:NOPE], kv_lat[:, k, :], k == 0, k == 1)
                    last.then_inc(qk_ready, 1)
                    for k in range(3):
                        last = mm(ps[0:ROPE, 1, 0:T], wq[:, k, NOPE:QK], q_lat[:, k, :], k == 0, k == 2)
                    last.then_inc(qr_ready, 1)
                    pe.wait_ge(merged_ready, done + 1)
                    for t in range(TT):
                        for k in range(2):
                            last = mm(ps[:, 2, t * P:(t + 1) * P], kv_lat[:, k, t * P:(t + 1) * P], wkv[:, k, NOPE:], k == 0, k == 1)
                    last.then_inc(v_ready, 1)
                    pe.wait_ge(u_done, done + 1)
                    conv_tile(0, ps[:, 5, 0:T])
                    pe.wait_ge(sq_ready, done + 1)
                    pe.wait_ge(max_ready, done + 1)
                    mm(ps[:, 3, 0:T], ones[:], k_sq, True, False)
                    mm(ps[:, 3, 0:T], ones[0:ROPE, :], k_rope_sq[:], False, True).then_inc(kss_ready, 1)
                    for t in range(TT):
                        mm(ps[:, 4, t:t + 1], q_sq[:, t * P:(t + 1) * P], ones[:, 0:1], True, False)
                        last = mm(ps[:, 4, t:t + 1], qr_sq[:, t * P:(t + 1) * P], ones[0:ROPE, 0:1], False, True)
                    last.then_inc(qss_ready, 1)
                    pe.wait_ge(qx_ready, done + 1)
                    mm(ps[:, 1, T:2 * T], co("swap", ROPE), q_x, True, True).then_inc(swap_ready, 1)
                    conv_tile(1, ps[:, 5, T:2 * T]).then_inc(zxc_ready, 1)
                    pe.wait_ge(kq_ready, done + 2)
                    pe.wait_ge(rk_sqrt, done + 1)
                    mm(ps[:, 3, 0:P], q_n[:, 0:P], k_n[:, 0:P], True, False)
                    mm(ps[:, 3, 0:P], q_r[:, 0:P], k_r[:, 0:P], False, True)
                    mm(ps[:, 3, P:P + T], q_n[:, P:T], k_n, True, False)
                    mm(ps[:, 3, P:P + T], q_r[:, P:T], k_r, False, True).then_inc(s_ready, 1)
                    pe.wait_ge(ada_landed[3], i * 32 + (16 * half + 32))
                    ada_item(ada_beside, ps[:, 0, 0:P]).then_inc(ada_done, 1)
                    pe.wait_ge(y_done, done + 1)
                    conv_tile(2, ps[:, 6, 0:T])
                    conv_tile(3, ps[:, 6, T:2 * T]).then_inc(zbg_ready, 1)
                    pe.wait_ge(ada_copied, done + 2)
                    nc.tensor.transpose(ps[:, 0, P:2 * P], ada_rows, ident).then_inc(ada_turned, 1)
                    pe.wait_ge(p_ready, done + 1)
                    nc.tensor.transpose(ps[:, 4, 0:P], probs[:, 0:P], ident)
                    nc.tensor.transpose(ps[:, 4, P:2 * P], probs[:, P:2 * P], ident)
                    nc.tensor.transpose(ps[:, 4, 2 * P:3 * P], probs[:, 2 * P:3 * P], ident).then_inc(pT_ready, 1)
                    conv_tile(4, ps[:, 7, 0:T]).then_inc(zgm_ready, 1)
                    pe.wait_ge(pT_copied, done + 1)
                    mm(ps[:, 2, T:2 * T], v_sb[:, 0, :], pT[:, 0:T], True, False)
                    mm(ps[:, 2, T + P:2 * T], v_sb[:, 1, :], pT[:, T:T + P], False, True).then_inc(o_ready, 1)

            pe.wait_ge(merged_ready, HEADS + 1)
            for a in range(2):
                slot = (WO0 + a) % 2
                pe.wait_ge(mix_landed[slot], 16 * ((WO0 + a) // 2 + 1))
                w = wmix[:, slot, 0:WO_COLS].rearrange("p (m k c) -> p m k c", m=4, k=KT)
                for m in range(4):
                    for k in range(KT):
                        last = mm(ps[:, 1 + 2 * a + m // 2, (m % 2) * T:(m % 2 + 1) * T], w[:, m, k, :], merged[:, k, :], k == 0, k == KT - 1)
                last.then_inc(wo_ready, 1)
            for k in range(KT):
                if k % 4 == 0:
                    pe.wait_ge(x2sq_ready, k // 4 + 1)
                last = mm(ps[:, 5, 0:T], ones[:], hT[:, k, :], k == 0, k == KT - 1)
            last.then_inc(x2ss_ready, 1)

            pe.wait_ge(h2_ready, KT)
            a0 = SMALL["w_router"][0]
            for t in range(TT):
                for k in range(KT):
                    last = mm(ps[:, 6, 64 * t:64 * t + 36], hT[:, k, t * P:(t + 1) * P], small[:, a0 + 36 * k:a0 + 36 * k + 36], k == 0, k == KT - 1)
            last.then_inc(lg_ready, 1)
            for b in range(4):
                for q in range(4):
                    last = nc.tensor.transpose(ps[:, 1 + b, q * P:(q + 1) * P], hT[:, (b % 2) * 4 + q, (b // 2) * P:(b // 2 + 1) * P], ident)
                last.then_inc(h2r_ready, 1)
            pe.wait_ge(onehot_ready, 1)
            mm(ps[:, 0, 0:32], before, oh[:, 2, 0, :], True, True)
            mm(ps[:, 0, 32:64], ones[:], oh[:, 2, 0, :], True, False)
            mm(ps[:, 0, 32:64], before, oh[:, 2, 1, :], False, True)
            mm(ps[:, 0, 64:96], ones[:], oh[:, 2, 0, :], True, False)
            mm(ps[:, 0, 64:96], ones[:], oh[:, 2, 1, :], False, True).then_inc(rank_ready, 1)
            pe.wait_ge(h2r_copied, 4)
            pe.wait_ge(wslot_ready, 1)
            mm(ps[:, 1, 0:P], ones[:], diag_win, True, True).then_inc(wrow_ready, 1)

            def gather(n):
                pe.wait_ge(sel_win_ready, n + 1)
                for t in range(TT):
                    for q in range(4):
                        last = mm(ps[q * WIN:(q + 1) * WIN, 3, 0:T], sel_win[:, t, :], h2_rows[:, t, q * T:(q + 1) * T], t == 0, t == TT - 1)
                last.then_inc(rows_ready, 1)

            def turn_rows(n):
                pe.wait_ge(rows_copied, n + 1)
                nc.tensor.transpose(ps[:, 3, T:T + P], rows_sb[:, 0:P], ident)
                nc.tensor.transpose(ps[:, 3, T + P:2 * T], rows_sb[:, P:T], ident).then_inc(rows_turned, 1)

            def turn_down(n):
                pe.wait_ge(y_stored, n + 1)
                pe.wait_ge(down_copied, n + 1)
                nc.tensor.transpose(ps[:, 4, 0:P], d_sb[:, 0:P], ident)
                nc.tensor.transpose(ps[:, 4, P:2 * P], d_sb[:, P:2 * P], ident).then_inc(down_turned, 1)

            def window(place, use, n, first=False):
                wgu = ex_place[place][:, 0:GU_COLS].rearrange("p (k c) -> p k c", k=KT)
                wdn = ex_place[place][:, GU_COLS:].rearrange("p (f c) -> p f c", f=2)
                pe.wait_ge(gu_landed[place], use)
                pe.wait_ge(xw_ready, n + 1)
                for k in range(KT):
                    for q in range(4):
                        last = mm(ps[q * WIN:(q + 1) * WIN, 0, 0:P], xw[:, k, :], wgu[:, k, q * P:(q + 1) * P], k == 0, k == KT - 1)
                last.then_inc(gu_ready, 1)
                if not first:
                    turn_down(n - 1)
                gather(n + 1)
                pe.wait_ge(gu_copied, n + 1)
                nc.tensor.transpose(ps[:, 1, 0:P], gu_sb, ident).then_inc(gu_turned, 1)
                turn_rows(n + 1)
                pe.wait_ge(down_landed[place], use)
                pe.wait_ge(act_done, n + 1)
                for f in range(2):
                    for q in range(4):
                        last = mm(ps[q * WIN:(q + 1) * WIN, 2, 0:T], act_t[:, f * WIN:(f + 1) * WIN], wdn[:, f, q * T:(q + 1) * T], f == 0, f == 1)
                last.then_inc(down_ready, 1)

            def expert(e, place, use, at, first=False):
                window(place, use, at, first)
                upto = windows_before(pe, e + 1)
                with pe.If(upto - at > 1):
                    with pe.Fori(1, upto - at) as w:
                        window(place, use, at + w)
                return upto

            pe.wait_ge(sel_win_ready, 1)
            gather(0)
            pe.wait_ge(diag_ready, 1)
            for b in range(2):
                last = mm(ps[:, 4 + b, :], ones[:], diag[:, 2 * b:2 * b + 2].rearrange("p a t n -> p (a t n)"), True, True)
            last.then_inc(spread_ready, 1)
            turn_rows(0)
            pe.wait_ge(table_ready, 1)
            pe.wait_ge(spread_copied, 1)
            ROUNDS = (EXPERTS - 2) // EX_SLOTS
            expert(0, 0, 16, windows_before(pe, 0), first=True)
            with pe.Fori(0, ROUNDS) as i:
                at = windows_before(pe, i * EX_SLOTS + 1)
                for s in range(1, EX_SLOTS + 1):
                    at = expert(i * EX_SLOTS + s, s % EX_SLOTS, i * 16 + 16 * (s // EX_SLOTS + 1), at)
            at = windows_before(pe, EXPERTS - 1)
            at = expert(EXPERTS - 1, 1, 16 * (ROUNDS + 1), at)
            turn_down(at - 1)

            pe.wait_ge(y_stored, at + 1)
            pe.wait_ge(comb_ready, 4)

            def turn(m):
                if m >= 2:
                    pe.wait_ge(yr_copied, m - 1)
                for t in range(4):
                    last = nc.tensor.transpose(ps[:, m % 2, t * P:(t + 1) * P], yT[:, m, t * P:(t + 1) * P], ident)
                last.then_inc(yr_ready, 1)

            turn(0)
            for m in range(KT):
                if m + 1 < KT:
                    turn(m + 1)
                pe.wait_ge(yr_copied, m + 1)
                if m >= 4:
                    pe.wait_ge(out_done, m - 3)
                for t in range(4):
                    c0 = (m % 2) * 512 + t * P
                    last = mm(ps[:, 4 + m % 4, 0:T], y_rows[:, c0:c0 + P], comb[:, t, :], t == 0, t == 3)
                last.then_inc(out_ready, 1)

        @block.vector
        def _(dve):
            v = nc.vector
            chain = [0, None]

            def step_value(k):
                return k if chain[1] is None else chain[1] + k

            def link(ins):
                chain[0] += 1
                ins.then_inc(dve_step, 1)
                dve.wait_ge(dve_step, step_value(chain[0]))

            v.memset(ones[:], 1.0).then_inc(setup_done, 1)
            v.memset(eps_1[:], EPS).then_inc(setup_done, 1)
            v.memset(eps_q[:], EPS * QK).then_inc(setup_done, 1)
            v.memset(u, 0.0).then_inc(setup_done, 1)

            C1 = 6.28125
            C2 = 0.0019350051879882812
            C3 = 2 * 3.141592653589793 - C1 - C2
            MAGIC = 1.5 * 2.0 ** 23
            dve.wait_ge(pos_landed, 16)
            dve.wait_ge(const_landed, 16)
            link(v.tensor_copy(posf, posi))
            link(v.tensor_scalar(posf, posf, co("inv_freq", ROPE), None, ALU.mult))
            for out, quarter in ((sin_t, 0.0), (cos_t, 0.25)):
                link(v.tensor_scalar(out[:], posf, 1.0 / (2 * PI), quarter, ALU.mult, ALU.add))
                link(v.tensor_scalar(out[:], out[:], MAGIC, None, ALU.add))
                link(v.tensor_scalar(out[:], out[:], MAGIC, None, ALU.subtract))
                link(v.scalar_tensor_tensor(rope_t, out[:], -C1, posf, ALU.mult, ALU.add))
                link(v.scalar_tensor_tensor(rope_t, out[:], -C2, rope_t, ALU.mult, ALU.add))
                link(v.scalar_tensor_tensor(rope_t, out[:], -C3, rope_t, ALU.mult, ALU.add))
                link(v.tensor_scalar(rope_t, rope_t, 2 * PI * quarter, None, ALU.add))
                last = v.tensor_scalar(out[:], rope_t, 3.141592, -3.141592, ALU.min, ALU.max)
                if quarter:
                    last.then_inc(angles_ready, 1)
                else:
                    link(last)

            dve.wait_ge(x_landed, 16)
            dve.wait_ge(r1_ready, 1)
            link(v.reciprocal(rms[:, T:2 * T], rms[:, 0:T]))
            link(v.tensor_tensor(hT, xT[:], rms[:, T:2 * T].unsqueeze(1).broadcast_to([P, KT, T]), ALU.mult))
            dve.wait_ge(small_landed, 16)
            dve.wait_ge(ada_turned, 1)
            link(v.tensor_tensor(mod[:, 0:16], ps[:, 1, :].rearrange("p (a c) -> p a c", c=WIN)[:, :, 0:1].rearrange("p a c -> p (a c)"), sm("b_ada", 0, 16), ALU.add))
            link(v.scalar_tensor_tensor(a12[:, 0, :], mod[:, 8:16], 1.0, sm("g1"), ALU.add, ALU.mult))
            for k in range(KT):
                v.tensor_scalar(hT[:, k, :], hT[:, k, :], a12[:, 0, k:k + 1], mod[:, k:k + 1], ALU.mult, ALU.add).then_inc(h_ready, 1)

            dve.wait_ge(lat_sq_ready, 1)
            v.tensor_scalar(k_r, ps[0:ROPE, 4, T:2 * T], sm("gk_rope", parts=ROPE), None, ALU.mult).then_inc(krope_ready, 1)
            dve.wait_ge(lat_rms_ready, 1)
            link(v.reciprocal(rms, rms))
            lat_ps = [ps[:, 1, 0:T], ps[:, 1, T:2 * T], ps[:, 2, 0:T], ps[:, 2, T:2 * T], ps[:, 4, 0:T]]
            for m in range(3):
                link(v.scalar_tensor_tensor(q_lat[:, m, :], lat_ps[m], sm("g_qa", m, 1), rms[:, 0:T], ALU.mult, ALU.mult))
            for m in range(2):
                link(v.scalar_tensor_tensor(kv_lat[:, m, :], lat_ps[3 + m], sm("g_kva", m, 1), rms[:, T:2 * T], ALU.mult, ALU.mult))
            v.tensor_tensor(stat[:, 15:16], sm("gq_nope"), sm("gk_nope"), ALU.mult).then_inc(lat_norm_ready, 1)
            dve.wait_ge(trig_ready, 1)
            dve.wait_ge(kswap_ready, 1)
            link(v.tensor_tensor(rope_t, ps[0:ROPE, 5, 0:T], sin_t[:], ALU.mult))
            link(v.tensor_tensor(k_rot[:], k_r, cos_t[:], ALU.mult))
            link(v.tensor_tensor(k_rot[:], k_rot[:], rope_t, ALU.add))

            for read_out in (mod_ready, kq_ready, merged_ready, u_done, max_ready, y_done):
                dve.sem_inc(read_out, 1)
            base, STEPS = chain[0], 14
            with dve.Fori(0, HEADS // 2) as i:
                for half in range(2):
                    n = i * 2 + (half + 1)
                    j = i * 2 + half
                    chain[0], chain[1] = base + half * STEPS, i * (2 * STEPS)
                    dve.wait_ge(sq_ready, n)
                    if half == 0:
                        dve.wait_ge(lat_norm_ready, 1)
                    v.tensor_scalar(q_x, ps[0:ROPE, 1, 0:T], sm("gq_rope", parts=ROPE), None, ALU.mult).then_inc(qx_ready, 1)
                    link(v.tensor_scalar(q_n, ps[:, 0, 0:T], stat[:, 15:16], None, ALU.mult))
                    dve.wait_ge(rk_sqrt, n)
                    link(v.reciprocal(rk, rk_s))
                    link(v.tensor_tensor(k_n, rk, ps[:, 0, T:2 * T], ALU.mult))
                    link(v.tensor_tensor(k_r, k_rot[:], rk[0:ROPE, :], ALU.mult))
                    dve.wait_ge(qx_ready, n)
                    link(v.tensor_tensor(q_r, q_x, cos_t[:], ALU.mult))
                    dve.wait_ge(swap_ready, n)
                    link(v.tensor_tensor(rope_t, sin_t[:], ps[0:ROPE, 1, T:2 * T], ALU.mult))
                    v.tensor_tensor(q_r, q_r, rope_t, ALU.add).then_inc(kq_ready, 1)
                    dve.wait_ge(zx_copied, n)
                    v.tensor_tensor(u[:, 2:T + 2], zx, ps[:, 5, T:2 * T], ALU.mult).then_inc(u_done, 1)
                    dve.wait_ge(u_done, n + 1)
                    c0 = SMALL["conv"][0]
                    link(v.tensor_scalar(conv_t, u[:, 0:T], small[:, bass.ds(j + c0, 1)], None, ALU.mult))
                    link(v.scalar_tensor_tensor(conv_t, u[:, 1:T + 1], small[:, bass.ds(j + (c0 + KT), 1)], conv_t, ALU.mult, ALU.add))
                    link(v.scalar_tensor_tensor(conv_t, u[:, 2:T + 2], small[:, bass.ds(j + (c0 + 2 * KT), 1)], conv_t, ALU.mult, ALU.add))
                    dve.wait_ge(qs_sqrt, n)
                    dve.wait_ge(s_ready, n)
                    v.reciprocal(stat[:, 2:4], stat[:, 0:2])
                    mask = co("mask")
                    v.tensor_tensor_reduce(out=scores[:, 0:P], in0=ps[:, 3, 0:P], in1=mask[:, P:T], scale=1.0, scalar=2 * LOW,
                                           op0=ALU.add, op1=ALU.max, accum_out=stat[:, 4:5])
                    link(v.tensor_tensor_reduce(out=scores[:, P:P + T], in0=ps[:, 3, P:P + T], in1=mask, scale=1.0, scalar=2 * LOW,
                                                op0=ALU.add, op1=ALU.max, accum_out=stat[:, 5:6]))
                    v.scalar_tensor_tensor(stat[:, 6:8], stat[:, 4:6], -1.0, stat[:, 2:4], ALU.mult, ALU.mult).then_inc(max_ready, 1)
                    dve.wait_ge(exp_done, n)
                    link(v.reciprocal(stat[:, 10:12], stat[:, 8:10]))
                    link(v.tensor_scalar(probs[:, 0:P], probs[:, 0:P], stat[:, 10:11], None, ALU.mult))
                    v.tensor_scalar(probs[:, P:P + T], probs[:, P:P + T], stat[:, 11:12], None, ALU.mult).then_inc(p_ready, 1)
                    dve.wait_ge(conv_gate_ready, n)
                    link(v.scalar_tensor_tensor(y_conv, ps[:, 6, 0:T], 0.5, conv_t, ALU.mult, ALU.mult))
                    v.scalar_tensor_tensor(y_conv, t_gate, 1.0, y_conv, ALU.add, ALU.mult).then_inc(y_done, 1)
                    dve.wait_ge(ada_turned, n + 1)
                    v.tensor_tensor(mod[:, bass.ds(i * 8 + (half * 4 + 16), 4)], ps[:, 0, P:2 * P].rearrange("p (a c) -> p a c", c=WIN)[:, :, 0:1].rearrange("p a c -> p (a c)"),
                                    small[:, bass.ds(i * 8 + (half * 4 + 16 + SMALL["b_ada"][0]), 4)], ALU.add).then_inc(mod_ready, 1)
                    dve.wait_ge(mla_gate_ready, n)
                    dve.wait_ge(o_ready, n)
                    dve.wait_ge(y_done, n + 1)
                    link(v.scalar_tensor_tensor(o_t, m_gate, 1.0, ps[:, 2, T:2 * T], ALU.add, ALU.mult))
                    v.scalar_tensor_tensor(merged[:, bass.ds(j, 1), :].rearrange("p a n -> p (a n)"), o_t, 0.5, y_conv, ALU.mult, ALU.add).then_inc(merged_ready, 1)
                    used = chain[0] - (base + half * STEPS)
                    assert used == STEPS, used
            chain[0], chain[1] = base + HEADS * STEPS, None

            dve.wait_ge(mod_ready, HEADS + 1)
            link(v.scalar_tensor_tensor(a12[:, 1, :], mod[:, 32:40], 1.0, sm("g2"), ALU.add, ALU.mult))
            for a in range(2):
                dve.wait_ge(wo_ready, a + 1)
                for m in range(4):
                    last = v.scalar_tensor_tensor(xT[:, 4 * a + m, :], ps[:, 1 + 2 * a + m // 2, (m % 2) * T:(m % 2 + 1) * T],
                                                  mod[:, 16 + 4 * a + m:17 + 4 * a + m], xT[:, 4 * a + m, :], ALU.mult, ALU.add)
                last.then_inc(x2_ready, 1)
            dve.wait_ge(x2_ready, 2)
            dve.wait_ge(r2_ready, 1)
            link(v.reciprocal(r2, r2s))
            for k in range(KT):
                v.scalar_tensor_tensor(hT[:, k, :], xT[:, k, :], a12[:, 1, k:k + 1], r2, ALU.mult, ALU.mult).then_inc(h2_scaled, 1)

            dve.wait_ge(lg_ready, 1)
            logits_ps = ps[:, 6, 0:128].rearrange("p (t n) -> p t n", t=TT)[:, :, 0:36]
            link(v.tensor_tensor(lg, logits_ps, sm("b_router").unsqueeze(1).broadcast_to([P, TT, 36]), ALU.add))
            G = [P, TT, GROUPS]
            E = [P, TT, PER_GROUP]
            G4 = [P, GROUPS, PER_GROUP]

            def b(ap, shape):
                return ap.unsqueeze(2).broadcast_to(shape)

            def first_of_max(values, number, top, tmp, onehot, shape, idx):
                link(v.tensor_reduce(top, values, AX_X, ALU.max))
                link(v.tensor_tensor(tmp, values, b(top, shape), ALU.is_equal))
                link(v.tensor_tensor(tmp, tmp, number, ALU.mult))
                link(v.tensor_reduce(idx, tmp, AX_X, ALU.min))
                link(v.tensor_tensor(onehot, number, b(idx, shape), ALU.is_equal))

            g_no = co("group_no").unsqueeze(1).broadcast_to(G)
            e_no = co("expert_no").unsqueeze(1).broadcast_to(E)
            lg_g = lg[:, :, 0:GROUPS]
            first_of_max(lg_g, g_no, s_work[:, 0, :], g_work[:, 0], g_work[:, 2], G, s_work[:, 1, :])
            v.tensor_tensor(g_work[:, 1], lg_g, b(s_work[:, 0, :], G), ALU.subtract).then_inc(gdiff_ready, 1)
            for t in range(TT):
                link(v.tensor_tensor(oh[:, 3, t, :].rearrange("p (g e) -> p g e", g=GROUPS),
                                     lg[:, t, GROUPS:].rearrange("p (g e) -> p g e", g=GROUPS),
                                     g_work[:, 2, t, :].unsqueeze(2).broadcast_to(G4), ALU.mult))
                link(v.tensor_reduce(e_work[:, 0, t, :], oh[:, 3, t, :].rearrange("p (g e) -> p e g", g=GROUPS), AX_X, ALU.add))
            first_of_max(e_work[:, 0], e_no, s_work[:, 2, :], e_work[:, 1], e_work[:, 2], E, s_work[:, 3, :])
            link(v.scalar_tensor_tensor(e_work[:, 3].rearrange("p t n -> p (t n)"), e_work[:, 2].rearrange("p t n -> p (t n)"), LOW,
                                        e_work[:, 0].rearrange("p t n -> p (t n)"), ALU.mult, ALU.add))
            first_of_max(e_work[:, 3], e_no, s_work[:, 4, :], e_work[:, 1], e_work[:, 4], E, s_work[:, 3, :])
            v.tensor_tensor(s_work[:, 5, :], s_work[:, 4, :], s_work[:, 2, :], ALU.subtract).then_inc(ediff_ready, 1)
            for c, e in ((0, 2), (1, 4)):
                for t in range(TT):
                    link(v.tensor_tensor(oh[:, c, t, :].rearrange("p (g e) -> p g e", g=GROUPS),
                                         g_work[:, 2, t, :].unsqueeze(2).broadcast_to(G4),
                                         e_work[:, e, t, :].unsqueeze(1).broadcast_to(G4), ALU.mult))
            v.tensor_tensor(oh[:, 2], oh[:, 0], oh[:, 1], ALU.add).then_inc(onehot_ready, 1)
            dve.wait_ge(gexp_ready, 1)
            link(v.tensor_reduce(s_work[:, 7, :], g_work[:, 1], AX_X, ALU.add))
            dve.wait_ge(eexp_ready, 1)
            link(v.scalar_tensor_tensor(s_work[:, 8, :], s_work[:, 6, :], 1.0, s_work[:, 7, :], ALU.add, ALU.mult))
            link(v.reciprocal(s_work[:, 8, :], s_work[:, 8, :]))
            link(v.tensor_tensor(s_work[:, 9, :], s_work[:, 8, :], s_work[:, 6, :], ALU.mult))
            dve.wait_ge(rank_ready, 1)
            link(v.tensor_copy(cnt, ps[:, 0, 64:96]))
            link(v.tensor_tensor_scan(incl, ones[:, 0:EXPERTS], cnt, 0.0, ALU.mult, ALU.add))
            link(v.tensor_tensor(offf, incl, cnt, ALU.subtract))
            link(v.tensor_tensor(pos_e, ps[:, 0, 0:64].rearrange("p (t n) -> p t n", t=TT), offf.unsqueeze(1).broadcast_to([P, TT, EXPERTS]), ALU.add))
            for c in range(2):
                link(v.tensor_tensor(oh[:, 3], oh[:, c], pos_e, ALU.mult))
                link(v.tensor_reduce(s_work[:, 10 + c, :], oh[:, 3], AX_X, ALU.add))
            link(v.tensor_scalar(wins[:, 0:EXPERTS], cnt, 1.0, 1.0 / WIN, ALU.max, ALU.mult))
            link(v.tensor_scalar(wins[:, 0:EXPERTS], wins[:, 0:EXPERTS], 0.5 - 0.5 / WIN, MAGIC, ALU.add, ALU.add))
            link(v.tensor_scalar(wins[:, 0:EXPERTS], wins[:, 0:EXPERTS], MAGIC, None, ALU.subtract))
            E1 = EXPERTS
            upto_e, at_e, in_e, val_e = wins[:, 2 * E1:3 * E1], wins[:, E1:2 * E1], wins[:, 3 * E1:4 * E1], wins[:, 4 * E1:5 * E1]
            link(v.tensor_tensor_scan(upto_e, ones[:, 0:E1], wins[:, 0:E1], 0.0, ALU.mult, ALU.add))
            link(v.tensor_tensor(at_e, upto_e, wins[:, 0:E1], ALU.subtract))
            v.tensor_copy(table[0:1, 0:E1], at_e[0:1, :])
            v.tensor_copy(table[0:1, E1:E1 + 1], upto_e[0:1, E1 - 1:E1])
            no = co("row_no")
            link(v.tensor_scalar(in_e, at_e, no, None, ALU.is_le))
            link(v.tensor_scalar(val_e, upto_e, no, None, ALU.is_gt))
            link(v.tensor_tensor(in_e, in_e, val_e, ALU.mult))
            link(v.scalar_tensor_tensor(val_e, at_e, -float(WIN), offf, ALU.mult, ALU.add))
            link(v.scalar_tensor_tensor(val_e, in_e, 1.0, val_e, ALU.mult, ALU.mult))
            link(v.tensor_reduce(wins[:, 5 * E1:5 * E1 + 1], val_e, AX_X, ALU.add))
            first_col = wins[:, 5 * E1 + 1:5 * E1 + 2]
            link(v.scalar_tensor_tensor(first_col, no, float(WIN), wins[:, 5 * E1:5 * E1 + 1], ALU.mult, ALU.add))
            link(v.tensor_scalar(first_col, first_col, float(SLOTS), None, ALU.min))
            v.tensor_scalar(diag_win, ident, first_col, None, ALU.mult).then_inc(wslot_ready, 1)
            slot_no = co("slot_no")
            for t in range(TT):
                link(v.tensor_scalar(sel[:, t, :], slot_no, s_work[:, 10, t:t + 1], None, ALU.is_equal))
                v.scalar_tensor_tensor(sel[:, t, :], slot_no, s_work[:, 11, t:t + 1], sel[:, t, :], ALU.is_equal, ALU.add).then_inc(sel_ready, 1)
            dve.wait_ge(wrow_ready, 1)
            v.tensor_copy(table[0:1, EXPERTS + 1:], ps[0:1, 1, 0:NW]).then_inc(table_ready, 1)
            dve.wait_ge(h2r_ready, 4)
            for c, col in enumerate((10, 11, 8, 9)):
                for t in range(TT):
                    last = v.tensor_scalar(diag[:, c, t, :], ident, s_work[:, col, t:t + 1], None, ALU.mult)
            last.then_inc(diag_ready, 1)
            dve.wait_ge(table_ready, 1)
            xw_ps = ps[:, 3, T:2 * T].rearrange("p (h q n) -> p q h n", h=2, q=4)
            xw_v = xw.rearrange("p (q h) n -> p q h n", h=2)
            dve.wait_ge(rows_ready, 2)
            v.tensor_copy(rows_sb, ps[:, 3, 0:T]).then_inc(rows_copied, 1)
            dve.wait_ge(rows_turned, 1)
            v.tensor_copy(xw_v, xw_ps).then_inc(xw_ready, 1)
            dve.wait_ge(spread_copied, 1)
            for c in range(4):
                row = co("row_no") if c == 0 else wins[:, 5 * E1 + 2:5 * E1 + 3]
                if c:
                    link(v.tensor_scalar(row, co("row_no"), float(c * P), None, ALU.add))
                v.scalar_tensor_tensor(comb[:, c, :], spread[:, 0, :], row, spread[:, 2, :], ALU.is_equal, ALU.mult)
                link(v.scalar_tensor_tensor(comb_b, spread[:, 1, :], row, spread[:, 3, :], ALU.is_equal, ALU.mult))
                v.tensor_tensor(comb[:, c, :], comb[:, c, :], comb_b, ALU.add).then_inc(comb_ready, 1)
                dve.wait_ge(comb_ready, c + 1)
            with dve.Fori(0, windows_before(dve, EXPERTS)) as n:
                dve.wait_ge(gu_ready, n + 1)
                v.tensor_copy(gu_sb, ps[:, 0, 0:P]).then_inc(gu_copied, 1)
                dve.wait_ge(rows_ready, n + 3)
                v.tensor_copy(rows_sb, ps[:, 3, 0:T]).then_inc(rows_copied, 1)
                dve.wait_ge(silu_done, n + 1)
                v.tensor_tensor(act_t, silu_t, ps[:, 1, 2 * WIN:4 * WIN], ALU.mult).then_inc(act_done, 1)
                dve.wait_ge(rows_turned, n + 2)
                v.tensor_copy(xw_v, xw_ps).then_inc(xw_ready, 1)
            for m in range(KT):
                dve.wait_ge(out_ready, m + 1)
                v.scalar_tensor_tensor(xT[:, m, :], ps[:, 4 + m % 4, 0:T], mod[:, 40 + m:41 + m], xT[:, m, :], ALU.mult, ALU.add).then_inc(out_done, 1)


def constants():
    import numpy as np
    c = np.zeros((P, N_CONST), np.float32)

    def put(name, a):
        at, w = CONST[name]
        c[0:a.shape[0], at:at + w] = a

    put("ident", np.eye(P, dtype=np.float32))
    r = np.arange(P)
    put("before", (r[:, None] < r[None, :]).astype(np.float32))
    swap = np.zeros((ROPE, ROPE), np.float32)
    h = ROPE // 2
    for m in range(h):
        swap[m + h, m] = -1.0
        swap[m, m + h] = 1.0
    put("swap", np.concatenate([swap, swap], axis=1))
    put("slot_no", np.broadcast_to(np.arange(SELW, dtype=np.float32), (P, SELW)))
    mask = np.zeros((P, T), np.float32)
    mask[0:CHUNK, T - CHUNK:] = LOW
    put("mask", mask)
    put("group_no", np.broadcast_to(np.arange(GROUPS, dtype=np.float32) - 100, (P, GROUPS)))
    put("expert_no", np.broadcast_to(np.arange(PER_GROUP, dtype=np.float32) - 100, (P, PER_GROUP)))
    put("row_no", np.arange(P, dtype=np.float32)[:, None])
    inv = np.float32(10000.0) ** (-np.arange(0, ROPE, 2, dtype=np.float32) / np.float32(ROPE))
    put("inv_freq", np.concatenate([inv, inv]).astype(np.float32)[:, None])
    return c


def kernel(**inputs):
    import numpy as np
    import concourse.bacc as bacc
    from concourse.bass_utils import run_bass_kernel_spmd as run

    a = {k: np.asarray(v) for k, v in inputs.items()}

    def cols(x):
        return x.reshape(-1, P).T

    def tiles(w, m):
        return w.reshape(w.shape[0] // P, P, m, P).transpose(1, 2, 0, 3).reshape(P, -1)

    def kcols(w):
        return w.reshape(w.shape[0] // P, P, -1).transpose(1, 0, 2).reshape(P, -1)

    small = np.zeros((P, N_SMALL), np.float32)

    def put(name, x):
        at, w = SMALL[name]
        small[0:x.shape[0], at:at + w] = x

    put("b_ada", cols(a["b_ada"][0]))
    put("g1", cols(a["norm1_g"][0]))
    put("g2", cols(a["norm2_g"][0]))
    put("c", cols(a["c"][0]))
    put("g_qa", cols(a["q_a_norm_g"][0]))
    put("g_kva", cols(a["kv_a_norm_g"][0]))
    put("gq_nope", a["q_norm_g"][0, :NOPE, None])
    put("gk_nope", a["k_norm_g"][0, :NOPE, None])
    put("gq_rope", a["q_norm_g"][0, NOPE:, None])
    put("gk_rope", a["k_norm_g"][0, NOPE:, None])
    put("conv", a["conv_w"][0].reshape(3 * KT, P).T)
    put("b_router", np.broadcast_to(np.concatenate([a["b_router_group"][0], a["b_router_expert"][0]]), (P, 36)))
    put("w_router", kcols(np.concatenate([a["w_router_group"][0], a["w_router_expert"][0]], axis=1)))

    w_in = a["w_in"][0]
    lat0 = 3 * D
    rope0 = lat0 + QL + KVL
    gc0 = rope0 + ROPE
    lat = np.concatenate([tiles(w_in[:, lat0:rope0], LAT_TILES), kcols(w_in[:, rope0:gc0])], axis=1)
    mix = []
    for j in range(HEADS):
        parts = [tiles(w_in[:, o + j * P:o + (j + 1) * P], 1) for o in (0, 2 * D, D, gc0, gc0 + D)]
        parts.append(kcols(a["w_q_b"][0][:, j * QK:(j + 1) * QK]))
        parts.append(kcols(a["w_kv_b"][0][:, j * 256:(j + 1) * 256]))
        mix.append(np.concatenate(parts, axis=1))
    wa = a["w_ada"][0]
    ada = np.stack([kcols(wa[:, n * 512:(n + 1) * 512]) for n in range(ADA_ITEMS)])
    wo = np.stack([tiles(a["w_o"][0][:, n * 512:(n + 1) * 512], 4) for n in range(2)])
    gate = a["w_exp_gate"][0].reshape(EXPERTS, KT, P, FF)
    up = a["w_exp_up"][0].reshape(EXPERTS, KT, P, FF)
    gate_up = np.concatenate([gate, up], axis=3).transpose(0, 2, 1, 3).reshape(EXPERTS, P, -1)
    down = a["w_exp_down"][0].reshape(EXPERTS, FF // P, P, D).transpose(0, 2, 1, 3).reshape(EXPERTS, P, -1)
    arrays = {
        "xT": a["x"][0].T.reshape(KT, P, T).transpose(1, 0, 2),
        "pos": np.broadcast_to(a["positions"], (ROPE, T)),
        "small": small,
        "const": constants(),
        "ada": ada,
        "lat": lat,
        "mix": np.stack(mix),
        "wo": wo,
        "gu": gate_up,
        "down": down,
    }
    arrays = {"in_" + k: np.ascontiguousarray(v) for k, v in arrays.items()}
    nc = bacc.Bacc("TRN2", target_bir_lowering=False, num_devices=1)
    aps = [nc.dram_tensor(k, v.shape, mybir.dt.from_np(v.dtype), kind="ExternalInput").ap() for k, v in arrays.items()]
    out = nc.dram_tensor("out_yT", (KT, P, T), F32, kind="ExternalOutput").ap()
    block_kernel(nc, *aps, out)
    r = run(nc, [arrays], core_ids=[0])
    y = np.asarray(r.results[0]["out_yT"])
    return np.ascontiguousarray(y.reshape(D, T).T).reshape(1, T, D)
```
